# Optimizing a Trainium2 kernel written in Bass

```python
import jax
import jax.numpy as jnp
from jax import lax
import numpy as np

D_MODEL = 1024
BATCH = 1
SEQ = 1024
DEPTH = 1

D_MIX = D_MODEL
D_ATTN = D_MIX // 2
D_HGRN = D_MIX - D_ATTN
ATTN_HEAD_DIM = 64
N_ATTN_HEADS = D_ATTN // ATTN_HEAD_DIM
HGRN_EXPAND = 128
N_HGRN_HEADS = D_HGRN // HGRN_EXPAND
HGRN_VDIM = D_HGRN // N_HGRN_HEADS
D_FF = 128 * ((8 * D_MODEL // 3 + 127) // 128)
N_MOD = 9
Q_BLOCK = 128
HGRN_CHUNK = 64
FFN_RES = 0.5
EPS = 1e-6
IN_SIZES = (D_ATTN, D_ATTN, D_ATTN, N_ATTN_HEADS, D_HGRN, D_HGRN, D_HGRN, D_HGRN)
N_IN = sum(IN_SIZES)

kernel_name = "fox_hgrn2_macaron_adaln_hybrid"

def _rms(x, g):
    xf = x.astype(jnp.float32)
    y = xf * lax.rsqrt(jnp.mean(xf * xf, axis=-1, keepdims=True) + EPS)
    return (y * g.astype(jnp.float32)).astype(x.dtype)

def _modulate(x, g, shift, scale):
    return _rms(x, g) * (1 + scale[:, None, :]) + shift[:, None, :]

def _swiglu(h, w_in, w_out):
    gate, up = jnp.split(h @ w_in, 2, axis=-1)
    return (jax.nn.silu(gate) * up) @ w_out

def _forgetting_attention(q, k, v, fg_logit, q_g, k_g):
    B, S, H, Dh = q.shape
    q = _rms(q, q_g).transpose(0, 2, 1, 3)
    k = _rms(k, k_g).transpose(0, 2, 1, 3)
    v = v.transpose(0, 2, 1, 3)
    logf = jax.nn.log_sigmoid(fg_logit.astype(jnp.float32))
    F = jnp.cumsum(logf, axis=1).transpose(0, 2, 1)
    scale = Dh ** -0.5
    outs = []
    for blk in range(S // Q_BLOCK):
        q0 = blk * Q_BLOCK
        L = q0 + Q_BLOCK
        s = jnp.einsum('bhqd,bhkd->bhqk', q[:, :, q0:L], k[:, :, :L],
                       preferred_element_type=jnp.float32) * scale
        s = s + F[:, :, q0:L, None] - F[:, :, None, :L]
        qpos = q0 + jnp.arange(Q_BLOCK)
        kpos = jnp.arange(L)
        s = jnp.where(kpos[None, :] <= qpos[:, None], s, -jnp.inf)
        p = jax.nn.softmax(s, axis=-1)
        outs.append(jnp.einsum('bhqk,bhkd->bhqd', p.astype(v.dtype), v[:, :, :L]))
    o = jnp.concatenate(outs, axis=2)
    return o.transpose(0, 2, 1, 3).reshape(B, S, H * Dh)

def _hgrn2(q, f_logit, i, lb):
    B, S, H, K = q.shape
    V = i.shape[-1]
    z = f_logit.astype(jnp.float32)
    lbf = lb.astype(jnp.float32).reshape(H, K)
    logf = jnp.logaddexp(jnp.log(lbf), jnp.log1p(-lbf) + jax.nn.log_sigmoid(z))
    kk = (1 - lbf) * jax.nn.sigmoid(-z)
    qf = jax.nn.silu(q.astype(jnp.float32))
    C = HGRN_CHUNK
    NC = S // C

    def to_chunks(t):
        return t.reshape(B, NC, C, H, t.shape[-1]).transpose(1, 0, 3, 2, 4)

    xs = (to_chunks(qf), to_chunks(kk), to_chunks(i.astype(jnp.float32)), to_chunks(logf))
    causal = jnp.tril(jnp.ones((C, C), dtype=bool))

    def step(state, inp):
        qb, kb, vb, gb = inp
        b = jnp.cumsum(gb, axis=2)
        o_inter = jnp.einsum('bhck,bhkv->bhcv', qb * jnp.exp(b), state)
        diff = b[:, :, :, None, :] - b[:, :, None, :, :]
        decay = jnp.exp(jnp.where(causal[:, :, None], diff, -jnp.inf))
        A = jnp.einsum('bhtk,bhsk,bhtsk->bhts', qb, kb, decay)
        o_intra = jnp.einsum('bhts,bhsv->bhtv', A, vb)
        b_last = b[:, :, -1:, :]
        new_state = (jnp.exp(b_last[:, :, 0, :])[..., None] * state
                     + jnp.einsum('bhsk,bhsv->bhkv', kb * jnp.exp(b_last - b), vb))
        return new_state, o_inter + o_intra

    s0 = jnp.zeros((B, H, K, V), jnp.float32)
    _, o = lax.scan(step, s0, xs)
    return o.transpose(1, 0, 3, 2, 4).reshape(B, S, H, V).astype(q.dtype)

def _hybrid_mixer(h, w_in, b_fgate, q_g, k_g, attn_out_g, lb, hgrn_out_g, w_out):
    B, S, _ = h.shape
    proj = h @ w_in
    idx = np.cumsum(IN_SIZES)[:-1].tolist()
    qa, ka, va, fg, qh, fh, ih, gh = jnp.split(proj, idx, axis=-1)
    heads_a = lambda t: t.reshape(B, S, N_ATTN_HEADS, ATTN_HEAD_DIM)
    o_a = _forgetting_attention(heads_a(qa), heads_a(ka), heads_a(va), fg + b_fgate, q_g, k_g)
    o_a = _rms(o_a, attn_out_g)
    heads_k = lambda t: t.reshape(B, S, N_HGRN_HEADS, HGRN_EXPAND)
    o_h = _hgrn2(heads_k(qh), heads_k(fh), ih.reshape(B, S, N_HGRN_HEADS, HGRN_VDIM), lb)
    o_h = _rms(o_h, hgrn_out_g.reshape(N_HGRN_HEADS, HGRN_VDIM)).reshape(B, S, D_HGRN)
    o_h = o_h * jax.nn.silu(gh)
    return jnp.concatenate([o_a, o_h], axis=-1) @ w_out

def setup_inputs(seed: int = 0) -> dict:
    key = jax.random.key(seed)
    ks = jax.random.split(key, 24)
    f32 = jnp.float32
    nrm = lambda k, shape, s: s * jax.random.normal(k, shape, f32)
    L = DEPTH
    w_in_mix = jnp.concatenate([
        nrm(ks[9], (L, D_MODEL, 3 * D_ATTN), D_MODEL ** -0.5),
        nrm(ks[10], (L, D_MODEL, N_ATTN_HEADS), 0.1 * D_MODEL ** -0.5),
        nrm(ks[11], (L, D_MODEL, 4 * D_HGRN), D_MODEL ** -0.5)], axis=-1)
    return {
        'x': nrm(ks[0], (BATCH, SEQ, D_MODEL), 1.0),
        'c': nrm(ks[1], (BATCH, D_MODEL), 1.0),
        'w_ada': nrm(ks[2], (L, D_MODEL, N_MOD * D_MODEL), 0.5 * D_MODEL ** -0.5),
        'b_ada': nrm(ks[3], (L, N_MOD * D_MODEL), 0.02),
        'g_norm1': 1 + nrm(ks[4], (L, D_MODEL), 0.02),
        'ffn1_w_in': nrm(ks[5], (L, D_MODEL, 2 * D_FF), D_MODEL ** -0.5),
        'ffn1_w_out': nrm(ks[6], (L, D_FF, D_MODEL), D_FF ** -0.5),
        'g_norm_mix': 1 + nrm(ks[7], (L, D_MODEL), 0.02),
        'w_in_mix': w_in_mix,
        'b_fgate': jax.random.uniform(ks[12], (L, N_ATTN_HEADS), f32, 1.0, 4.0),
        'q_norm_g': 1 + nrm(ks[13], (L, ATTN_HEAD_DIM), 0.02),
        'k_norm_g': 1 + nrm(ks[14], (L, ATTN_HEAD_DIM), 0.02),
        'attn_out_g': 1 + nrm(ks[15], (L, D_ATTN), 0.02),
        'hgrn_lb_logits': nrm(ks[16], (DEPTH + 1, D_HGRN), 0.1),
        'hgrn_out_g': 1 + nrm(ks[17], (L, D_HGRN), 0.02),
        'w_out_mix': nrm(ks[18], (L, D_MIX, D_MODEL), D_MIX ** -0.5),
        'g_norm2': 1 + nrm(ks[19], (L, D_MODEL), 0.02),
        'ffn2_w_in': nrm(ks[20], (L, D_MODEL, 2 * D_FF), D_MODEL ** -0.5),
        'ffn2_w_out': nrm(ks[21], (L, D_FF, D_MODEL), D_FF ** -0.5),
    }

def reference(x, c, w_ada, b_ada, g_norm1, ffn1_w_in, ffn1_w_out, g_norm_mix, w_in_mix,
              b_fgate, q_norm_g, k_norm_g, attn_out_g, hgrn_lb_logits, hgrn_out_g,
              w_out_mix, g_norm2, ffn2_w_in, ffn2_w_out):
    lb_all = jnp.cumsum(jax.nn.softmax(hgrn_lb_logits.astype(jnp.float32), axis=0), axis=0)
    cs = jax.nn.silu(c)
    for l in range(DEPTH):
        mod = cs @ w_ada[l] + b_ada[l]
        sh1, sc1, gt1, shm, scm, gtm, sh2, sc2, gt2 = jnp.split(mod, N_MOD, axis=-1)
        h = _modulate(x, g_norm1[l], sh1, sc1)
        x = x + FFN_RES * gt1[:, None, :] * _swiglu(h, ffn1_w_in[l], ffn1_w_out[l])
        h = _modulate(x, g_norm_mix[l], shm, scm)
        x = x + gtm[:, None, :] * _hybrid_mixer(h, w_in_mix[l], b_fgate[l], q_norm_g[l], k_norm_g[l],
                                                attn_out_g[l], lb_all[l], hgrn_out_g[l], w_out_mix[l])
        h = _modulate(x, g_norm2[l], sh2, sc2)
        x = x + FFN_RES * gt2[:, None, :] * _swiglu(h, ffn2_w_in[l], ffn2_w_out[l])
    return x


_drawn_inputs = setup_inputs


def setup_inputs(seed=0):
    import zlib

    import numpy as np

    out = dict(_drawn_inputs(seed))
    spreads = {}
    factors = {'g_norm1': 8.0,
     'g_norm_mix': 8.0,
     'q_norm_g': 8.0,
     'k_norm_g': 21.459,
     'attn_out_g': 64.0,
     'hgrn_lb_logits': 8.0,
     'hgrn_out_g': 26.635,
     'g_norm2': 32.779}
    for name, (base, spread) in spreads.items():
        noise = np.random.default_rng([zlib.crc32(name.encode()), seed]).standard_normal(out[name].shape)
        drawn = base * np.exp(spread * noise) if base else spread * noise
        out[name] = jnp.asarray(drawn.astype(out[name].dtype))
    for name, factor in factors.items():
        out[name] = (out[name] * factor).astype(out[name].dtype)
    return out
```

```python
from contextlib import ExitStack

import concourse.bass as bass
from concourse import mybir

ALU = mybir.AluOpType
ACT = mybir.ActivationFunctionType
AX_X = mybir.AxisListType.X
F32 = mybir.dt.float32
F32R = mybir.dt.float32r
BF16 = mybir.dt.bfloat16
U8 = mybir.dt.uint8

P = 128
BANK = 512
EPS = 1e-6
N_MOD = 9
SH1, SC1, GT1, SHM, SCM, GTM, SH2, SC2, GT2 = range(N_MOD)


def build(nc, x, c, w_ada, b_ada, g_norm1, ffn1_w_in, ffn1_w_out, g_norm_mix, w_in_mix, b_fgate,
          q_norm_g, k_norm_g, attn_out_g, hgrn_lb_logits, hgrn_out_g, w_out_mix, g_norm2,
          ffn2_w_in, ffn2_w_out, out):
    _, S, D = x.shape
    KD = D // P
    TT = S // P
    HALVES = S // BANK
    F = ffn1_w_out.shape[1]
    CF = F // P
    GROUPS = CF // 2
    assert CF == 2 * GROUPS and GROUPS % 2 == 1 and KD == 8 and TT == 8

    ROW_C = 0
    ROW_B = ROW_C + KD
    ROW_G = ROW_B + N_MOD * KD
    ROW_AG = ROW_G + 3 * KD
    ROW_HG = ROW_AG + 4
    ROW_LB = ROW_HG + 4
    ROW_Q = ROW_LB + 8
    ROW_K = ROW_Q + 1
    N_ROWS = ROW_K + 1

    DA = attn_out_g.shape[1]
    HD = q_norm_g.shape[1]
    NH = DA // HD
    PAIRS = DA // P
    NG = hgrn_out_g.shape[1] // P
    assert HD == 64 and PAIRS == NG == 4 and D == DA + NG * P
    LEVELS = [P >> (n + 1) for n in range(7)]
    MASKED = -1e30
    COL_Q, COL_K, COL_V, COL_FG = 0, DA, 2 * DA, 3 * DA
    COL_HQ = COL_FG + NH
    COL_HF, COL_HI, COL_HG = COL_HQ + NG * P, COL_HQ + 2 * NG * P, COL_HQ + 3 * NG * P

    PER_I = 7
    N_MIX_IN = 1 + 3 + PER_I * NG - 3
    U_FFN1 = 0
    U_MIX = 2 * CF
    U_FFN2 = U_MIX + N_MIX_IN + KD
    RAW_MIX = [CF + 1 + 1, CF + 1 + 1]
    RAW_PER_I = [4, 3]
    RAW_FFN2 = [RAW_MIX[k] + RAW_PER_I[k] * (NG - 1) + 2 + KD // 2 for k in range(2)]

    ctx = ExitStack()
    with ctx:
        sem = lambda name: ctx.enter_context(nc.semaphore(name))
        top = [nc.sbuf_base + (-nc.sbuf_base) % 32]

        def place(name, shape, dt=F32, at=None):
            n = {U8: 1, BF16: 2}.get(dt, 4)
            for k in shape[1:]:
                n *= k
            off = top[0] if at is None else at
            if at is None:
                top[0] += n + (-n) % 32
            t = nc.alloc_sbuf_tensor_at(name, shape, dt, offset=off)
            return t, off

        xT, x_at = place("xT", [P, KD, S])
        h_hi, h_at = place("h_hi", [P, KD, S], F32R)
        h_lo, _ = place("h_lo", [P, KD, S], F32R)
        raw, _ = place("raw", [P, 2, KD, P])
        w01_hi, _ = place("w01_hi", [P, 2, KD, P], F32R)
        w01_lo, _ = place("w01_lo", [P, 2, KD, P], F32R)
        w23_hi, mix_at = place("w23_hi", [P, 2, KD, P], F32R)
        w23_lo, _ = place("w23_lo", [P, 2, KD, P], F32R)
        w_hi = [w01_hi[:, 0], w01_hi[:, 1], w23_hi[:, 0], w23_hi[:, 1]]
        w_lo = [w01_lo[:, 0], w01_lo[:, 1], w23_lo[:, 0], w23_lo[:, 1]]
        raw2, _ = place("raw2", [P, D])
        w2_hi, w2_at = place("w2_hi", [P, 2, D], F32R)
        w2_lo, _ = place("w2_lo", [P, 2, D], F32R)
        act_hi0, _ = place("act_hi0", [P, 2, S], F32R)
        act_lo0, _ = place("act_lo0", [P, 2, S], F32R)
        act_hi1, act1_at = place("act_hi1", [P, 2, S], F32R)
        act_lo1, _ = place("act_lo1", [P, 2, S], F32R)
        act_hi, act_lo = [act_hi0, act_hi1], [act_lo0, act_lo1]
        gated, _ = place("gated", [P, S])
        ada_ring, _ = place("ada_ring", [P, 2, D])
        ada_acc, _ = place("ada_acc", [P, D])
        ada_end = top[0]
        ident, _ = place("ident", [P, P])
        ones, _ = place("ones", [P, P])
        cols, _ = place("cols", [P, N_ROWS])
        c_silu, _ = place("c_silu", [P, KD])
        mod, _ = place("mod", [P, N_MOD, KD])
        amp, _ = place("amp", [P, 3, KD])
        gate, _ = place("gate", [P, 3, KD])
        eps_col, _ = place("eps_col", [P, 1])
        ln_floor, _ = place("ln_floor", [P, 1])
        block_ones, _ = place("block_ones", [P, P])
        ident_bf, _ = place("ident_bf", [P, P], BF16)
        causal_bf, _ = place("causal_bf", [P, P], BF16)
        ident_u8, _ = place("ident_u8", [P, P], U8)
        level_u8, _ = place("level_u8", [P, len(LEVELS), P // 2], U8)
        lb, _ = place("lb", [P, NG])
        one_less_lb, _ = place("one_less_lb", [P, NG])
        lb_e, _ = place("lb_e", [P, 2, NG])
        q_gain, _ = place("q_gain", [P, 2])
        b_fg, _ = place("b_fg", [NH, 1])
        assert top[0] <= nc.sbuf_usable_end, (top[0], nc.sbuf_usable_end)

        K4 = 4 * S
        ov = lambda name, shape, dt, kb: place(name, shape, dt, at=mix_at + int(kb * 1024))[0]
        mixed = place("mixed", [P, KD, S], at=x_at)[0]
        q_hi, q_lo, k_hi, k_lo = [ov(n, [P, S], F32R, 4 * j) for j, n in enumerate(("q_hi", "q_lo", "k_hi", "k_lo"))]
        v_hi, v_lo = ov("v_hi", [P, TT, P], F32R, 16), ov("v_lo", [P, TT, P], F32R, 20)
        aug = ov("aug", [68, 2, S], F32R, 24)
        z_b, kk, qh, gh = [ov(n, [P, S], F32, 32 + 4 * j) for j, n in enumerate(("z_b", "kk", "qh", "gh"))]
        v_tok = ov("v_tok", [P, TT, P], F32, 48)
        stage = ov("stage", [P, S], F32, 52)
        probs = ov("probs", [P, 2, S], F32, 56)
        pT_hi, pT_lo = ov("pT_hi", [P, TT, P], F32R, 64), ov("pT_lo", [P, TT, P], F32R, 68)
        dec = ov("dec", [P, 2, S], F32, 56)
        q_up = ov("q_up", [P, S // 2], F32, 64)
        A = ov("A", [P, TT, P], F32, 66)
        qb = ov("qb", [P, S], F32, 70)
        kd = ov("kd", [P, TT, P], F32, 74)
        state = ov("state", [P, TT, P], F32, 78)
        neg_max, row_sum, row_inv = [ov(n, [P, 2], F32, 82 + j / 32) for j, n in enumerate(("neg_max", "row_sum", "row_inv"))]
        chunk_decay = ov("chunk_decay", [P, TT], F32, 83)
        fg_t, fg_l, fg_F, fg_one = [ov(n, [NH, S], F32, 68 + 4 * j) for j, n in enumerate(("fg_t", "fg_l", "fg_F", "fg_one"))]
        fg4 = ov("fg4", [NH, 4, S], F32R, 32)
        osq, osq_sum, orstd = ov("osq", [P, 2, S], F32, 0), ov("osq_sum", [P, S], F32, 8), ov("orstd", [P, S], F32, 12)
        assert mix_at + 84 * 1024 <= ada_end
        x_spill = nc.dram_tensor("x_spill", [P, KD, S], F32).ap()
        f_rows = nc.dram_tensor("f_rows", [NH, 2, 4, S], F32).ap()

        x_rows, _ = place("x_rows", [P, TT, D], at=h_at)
        ada_first, _ = place("ada_first", [P, KD, D], at=w2_at)
        sq, _ = place("sq", [P, 2, S], at=act1_at)
        sq_sum, _ = place("sq_sum", [P, S], at=act1_at + 8 * S)
        rstd, _ = place("rstd", [P, S], at=act1_at + 12 * S)
        rows, _ = place("rows", [P, P], at=act1_at)
        c_low = place("c_low", [P, P], at=mix_at + 512)[0]
        c_lvl = place("c_lvl", [P, len(LEVELS), P // 2], at=mix_at + 1024)[0]
        out_rows, _ = place("out_rows", [P, 2, TT, P], at=act1_at)

        ps = ctx.enter_context(nc.psum_tensor("ps", [P, 4, 2, BANK], F32))
        pair = lambda n: ps[:, n].rearrange("p h f -> p (h f)")

        s_rows = sem("rows_loaded")
        s_x = sem("x_loaded")
        s_const = sem("consts_built")
        s_colsT = sem("cols_transposed")
        s_cols = sem("cols_ready")
        s_csilu = sem("c_silu_ready")
        s_xt = sem("x_transposed")
        s_xT = sem("xT_copied")
        s_adaL0 = [sem(f"ada_first_loaded{k}") for k in range(KD)]
        s_adaL = [sem(f"ada_loaded{k}") for k in range(2)]
        s_adaA = sem("ada_tiles_added")
        s_adaP = sem("mod_summed")
        s_mod = sem("mod_read")
        s_gate = sem("gate_ready")
        s_unitL = [sem(f"unit_loaded{k}") for k in range(2)]
        s_unitHi = sem("unit_hi_written")
        s_unitLo = sem("unit_lo_written")
        s_unitUsed = sem("unit_used")
        s_outT = sem("out_transposed")
        s_outC = sem("out_copied")
        s_outS = [sem(f"out_stored{k}") for k in range(2)]

        class Norm:
            def __init__(self, n):
                self.n = n
                self.sq = sem(f"norm{n}_squared")
                self.added = sem(f"norm{n}_squares_added")
                self.summed = sem(f"norm{n}_partitions_summed")
                self.ln = sem(f"norm{n}_ln")
                self.rstd = sem(f"norm{n}_rstd")
                self.t = sem(f"norm{n}_scaled")
                self.hi = sem(f"norm{n}_h_hi")
                self.h = sem(f"norm{n}_h_ready")

        CONSTS = 8 + 3 * len(LEVELS)

        class Ffn:
            def __init__(self, n, unit0, raw0, norm, g, w_in, w_out, has_ada):
                self.raw0 = raw0
                self.n, self.unit0, self.norm, self.gate, self.has_ada = n, unit0, norm, g, has_ada
                self.w_in = w_in[0].rearrange("(k p) (s c j) -> p k s c j", p=P, s=2, j=P)
                self.w_out = w_out[0].rearrange("(c p) d -> c p d", p=P)
                self.w2_loaded = sem(f"ffn{n}_w2_loaded")
                self.w2_hi = sem(f"ffn{n}_w2_hi")
                self.w2_lo = sem(f"ffn{n}_w2_lo")
                self.up = sem(f"ffn{n}_up_done")
                self.silu = sem(f"ffn{n}_silu_done")
                self.act = sem(f"ffn{n}_gated")
                self.act_hi = sem(f"ffn{n}_act_hi")
                self.act_lo = sem(f"ffn{n}_act_lo")
                self.down = sem(f"ffn{n}_down_done")
                self.x = sem(f"ffn{n}_x_updated")

        s_spill = sem("x_spilled")
        s_back = [sem(f"x_back{d}") for d in range(KD)]
        s_small = sem("small_constants")
        s_lbe = sem("lb_steps")
        m_half = sem("mix_half_units_done")
        m_copied = sem("mix_halves_copied")
        fg_s = sem("fg_steps")
        fg_stored = sem("f_rows_stored")
        aug_loaded = sem("aug_loaded")
        a_sq = sem("qk_squared")
        a_sum = sem("qk_squares_summed")
        a_ln = sem("qk_ln")
        a_rstd = sem("qk_rstd")
        a_n = sem("qk_normed")
        a_hi = sem("qk_hi")
        a_lo = sem("qk_lo")
        a_vT = sem("v_transposed")
        a_vhi = sem("v_hi_written")
        a_vlo = sem("v_lo_written")
        t_S = sem("scores_done")
        t_max = sem("row_max_done")
        t_exp = sem("exp_done")
        t_inv = sem("row_inverse_done")
        t_P = sem("probs_scaled")
        t_T = sem("probs_transposed")
        t_hi = sem("pT_hi_written")
        t_lo = sem("pT_lo_written")
        t_PV = sem("pv_done")
        t_O = sem("attention_out_written")
        g_sig = sem("sigmoids_done")
        g_gates = sem("gates_done")
        g_ln = sem("log_f_done")
        g_b = sem("log_decays_summed")
        g_kd0 = sem("to_chunk_end")
        g_e = sem("chunk_exps_done")
        g_kdT = sem("kd_columns_ready")
        g_qb = sem("qb_ready")
        g_kdP = sem("kd_transposed")
        g_kd = sem("kd_copied")
        g_iT = sem("i_transposed")
        g_v = sem("v_tok_copied")
        g_zero = sem("A_zeroed")
        l_sub = sem("level_differences")
        l_exp = sem("level_exps")
        l_mul = sem("level_operands")
        l_P = sem("level_products")
        l_last = sem("last_level_product")
        l_cp = sem("level_copied")
        g_diag = sem("diagonal_product")
        g_diagC = sem("diagonal_copied")
        g_dS = sem("state_products")
        g_state = sem("states_ready")
        g_o = sem("hgrn_out_product")
        g_osq = sem("hgrn_out_squared")
        g_osum = sem("hgrn_out_summed")
        g_oln = sem("hgrn_out_ln")
        g_orstd = sem("hgrn_out_rstd")
        g_ot = sem("hgrn_out_scaled")
        g_mixed = sem("hgrn_mixed")
        n_sq = sem("attn_out_squared")
        n_add = sem("attn_out_squares_added")
        n_sum = sem("attn_out_summed")
        n_ln = sem("attn_out_ln")
        n_rstd = sem("attn_out_rstd")
        n_t = sem("attn_out_scaled")
        m_hi = sem("mixed_hi")
        m_lo = sem("mixed_lo")
        p_done = sem("w_out_product")
        p_x = sem("mix_x_updated")
        norms = [Norm(n) for n in range(3)]
        ffn1 = Ffn(1, U_FFN1, [0, 0], norms[0], 0, ffn1_w_in, ffn1_w_out, True)
        ffn2 = Ffn(2, U_FFN2, RAW_FFN2, norms[2], 2, ffn2_w_in, ffn2_w_out, False)
        ADA_FIRST = 3

        def group_segments(eng, f, body, after_ada=None):
            body(0, 0, f.has_ada)
            body(1, 1, f.has_ada)
            pairs = [(1, 3, f.has_ada), (3, GROUPS // 2, False)] if f.has_ada else [(1, GROUPS // 2, False)]
            for lo, hi, ada in pairs:
                with eng.Fori(lo, hi) as t:
                    body(2 * t, 0, ada)
                    body(2 * t + 1, 1, ada)
                if ada and after_ada:
                    after_ada(2 * hi)
            body(GROUPS - 1, 0, False)

        block = ctx.enter_context(nc.Block())

        @block.sync
        def _(sp):
            sp.dma_start(rows[ROW_C:ROW_B, :], c.rearrange("a (r j) -> (a r) j", j=P)).then_inc(s_rows, 16)
            sp.dma_start(rows[ROW_B:ROW_G, :], b_ada.rearrange("a (r j) -> (a r) j", j=P)).then_inc(s_rows, 16)
            for n, g in enumerate((g_norm1, g_norm_mix, g_norm2)):
                sp.dma_start(rows[ROW_G + n * KD:ROW_G + (n + 1) * KD, :],
                             g.rearrange("a (r j) -> (a r) j", j=P)).then_inc(s_rows, 16)
            sp.dma_start(rows[ROW_AG:ROW_HG, :], attn_out_g.rearrange("a (r j) -> (a r) j", j=P)).then_inc(s_rows, 16)
            sp.dma_start(rows[ROW_HG:ROW_LB, :], hgrn_out_g.rearrange("a (r j) -> (a r) j", j=P)).then_inc(s_rows, 16)
            sp.dma_start(rows[ROW_LB:ROW_Q, :], hgrn_lb_logits.rearrange("a (r j) -> (a r) j", j=P)).then_inc(s_rows, 16)
            for r, g in ((ROW_Q, q_norm_g), (ROW_K, k_norm_g)):
                for half in range(2):
                    sp.dma_start(rows[r:r + 1, 64 * half:64 * half + 64], g).then_inc(s_rows, 16)
            sp.dma_start(x_rows[:, :, :], x[0].rearrange("(t p) d -> p t d", p=P)).then_inc(s_x, 16)

            def load_unit(u, slot, src, behind=1):
                if not (isinstance(u, int) and u < 2):
                    sp.wait_ge(s_unitLo, u - behind)
                sp.dma_start(raw[:, slot], src).then_inc(s_unitL[slot], 16)

            def load_ffn_chunk(f, ch):
                for s in range(2):
                    load_unit(f.unit0 + 2 * ch + s, s, f.w_in[:, :, s, ch, :])

            load_ffn_chunk(ffn1, 0)
            with sp.Fori(1, CF) as ch:
                load_ffn_chunk(ffn1, ch)
            w_mix = w_in_mix[0].rearrange("(k p) n -> p k n", p=P)
            tiles = lambda c0: w_mix[:, :, c0:c0 + NG * P].rearrange("p k (i j) -> p k i j", j=P)
            tq, tk, tv, thf, thq, thg, thi = [tiles(c0) for c0 in (COL_Q, COL_K, COL_V, COL_HF, COL_HQ, COL_HG, COL_HI)]
            load_unit(U_MIX, 1, w_mix[:, :, COL_FG:COL_FG + P], behind=0)
            sp.wait_ge(ffn1.x, KD * GROUPS)
            sp.dma_start(x_spill, xT[:, :, :]).then_inc(s_spill, 16)
            for n, tl in enumerate((tq, tk, tv)):
                load_unit(U_MIX + 1 + n, n % 2, tl[:, :, 0, :])

            def load_round(i, last):
                u = U_MIX + 4 + PER_I * i
                for n, tl in enumerate((thf, thq, thg, thi)):
                    load_unit(u + n, n % 2, tl[:, :, i, :], behind=0 if n == 0 else 1)
                if not last:
                    for n, tl in enumerate((tq, tk, tv)):
                        load_unit(u + 4 + n, n % 2, tl[:, :, i + 1, :])

            with sp.Fori(0, NG - 1) as i:
                load_round(i, False)
            load_round(NG - 1, True)
            w_om = w_out_mix[0].rearrange("(k p) (d j) -> p k d j", p=P, j=P)
            for d in range(KD):
                load_unit(U_MIX + N_MIX_IN + d, d % 2, w_om[:, :, d, :])
                if d == 1:
                    sp.wait_ge(m_lo, KD)
                    for e in range(KD):
                        sp.dma_start(xT[:, e], x_spill[:, e]).then_inc(s_back[e], 16)
            with sp.Fori(0, CF) as ch:
                load_ffn_chunk(ffn2, ch)
            for k in range(2):
                sp.wait_ge(s_outS[k], 16 * (KD // 2))

        @block.gpsimd
        def _(pool):
            pool.memset(ident[:, :], 0.0)
            pool.memset(ones[:, :], 1.0)
            pool.memset(eps_col[:, :], EPS).then_inc(s_const, 1)
            pool.wait_ge(s_const, 1)
            pool.affine_select(out=ident[:, :], in_=ident[:, :], compare_op=ALU.not_equal, fill=1.0,
                               base=0, pattern=[[-1, P]], channel_multiplier=1).then_inc(s_const, 1)
            pool.memset(c_low[:, :], 0.0)
            pool.memset(c_lvl[:, :, :], 1.0)
            pool.memset(ln_floor[:, :], 1e-19).then_inc(s_const, 1)
            pool.wait_ge(s_const, 3)
            pool.memset(block_ones[:, :], 0.0).then_inc(s_const, 1)
            pool.wait_ge(s_const, 4)
            for e in range(2):
                pool.memset(block_ones[HD * e:HD * e + HD, HD * e:HD * e + HD], 1.0).then_inc(s_const, 1)
                pool.wait_ge(s_const, 5 + e)
            pool.wait_ge(s_const, 6)
            pool.affine_select(out=c_low[:, :], in_=c_low[:, :], compare_op=ALU.is_ge, fill=MASKED, base=0,
                               pattern=[[-1, P]], channel_multiplier=1).then_inc(s_const, 1)
            pool.wait_ge(s_const, 7)
            pool.tensor_copy(causal_bf[:, :], c_low[:, :])
            pool.tensor_copy(ident_bf[:, :], ident[:, :])
            pool.tensor_copy(ident_u8[:, :], ident[:, :]).then_inc(s_const, 1)
            pool.wait_ge(s_const, 8)
            for n, m in enumerate(LEVELS):
                v = c_lvl[:, n, :].rearrange("p (q r) -> p q r", r=m)
                nb = P // 2 // m
                pool.affine_select(out=v, in_=v, compare_op=ALU.is_ge, fill=0.0, base=0,
                                   pattern=[[-2 * m, nb], [0, m]], channel_multiplier=1).then_inc(s_const, 1)
                pool.wait_ge(s_const, 9 + 3 * n)
                pool.affine_select(out=v, in_=v, compare_op=ALU.is_ge, fill=0.0, base=m - 1,
                                   pattern=[[2 * m, nb], [0, m]], channel_multiplier=-1).then_inc(s_const, 1)
                pool.wait_ge(s_const, 10 + 3 * n)
                pool.tensor_copy(level_u8[:, n, :], c_lvl[:, n, :]).then_inc(s_const, 1)
                pool.wait_ge(s_const, 11 + 3 * n)
            pool.dma_start(b_fg[:, :], b_fgate.rearrange("a h -> h a")).then_inc(s_small, 16)
            ada = w_ada[0].rearrange("(k p) (v d) -> p k v d", p=P, v=N_MOD)
            for v in range(ADA_FIRST):
                for k in range(KD):
                    if v:
                        pool.wait_ge(s_adaA, KD * (v - 1) + k + 1)
                    pool.dma_start(ada_first[:, k, :], ada[:, k, v, :]).then_inc(s_adaL0[k], 16)

            def load_w2(f, ch):
                if not (isinstance(ch, int) and ch == 0):
                    pool.wait_ge(f.w2_lo, ch)
                pool.dma_start(raw2[:, :], f.w_out[ch]).then_inc(f.w2_loaded, 16)

            def group(g, parity, ada_on):
                if not (isinstance(g, int) and g == 0):
                    load_w2(ffn1, 2 * g - 2)
                    load_w2(ffn1, 2 * g - 1)
                if ada_on:
                    v = g + ADA_FIRST
                    for k in range(KD):
                        pool.wait_ge(s_adaA, KD * v + k - 1)
                        pool.dma_start(ada_ring[:, k % 2, :], ada[:, k, v, :]).then_inc(s_adaL[k % 2], 16)

            group_segments(pool, ffn1, group)
            load_w2(ffn1, CF - 2)
            load_w2(ffn1, CF - 1)
            pool.wait_ge(fg_stored, 16 * 8)
            aug_f = aug[:, :, :].bitcast(F32)

            def load_aug(i):
                for e in range(2):
                    pool.dma_start(aug_f[64 * e:64 * e + 4], f_rows.rearrange("(i e) s r t -> i e r s t", e=2)[i, e]
                                   ).then_inc(aug_loaded, 16)
            load_aug(0)
            pool.wait_ge(g_gates, 4)
            pool.memset(A[:, :, :], 0.0).then_inc(g_zero, 1)
            with pool.Fori(1, NG) as i:
                pool.wait_ge(t_S, 2 * TT * i)
                load_aug(i)
                pool.wait_ge(g_gates, 4 * (i + 1))
                pool.tensor_tensor(A[:, :, :], A[:, :, :], A[:, :, :], ALU.subtract).then_inc(g_zero, 1)
            pool.wait_ge(norms[2].rstd, 1)
            load_w2(ffn2, 0)
            with pool.Fori(1, CF) as ch:
                load_w2(ffn2, ch)

        @block.tensor
        def _(pe):
            def three_pass(dst, whi, wlo, mhi, mlo, start, stop):
                pe.matmul(dst, whi, mhi, start=start, stop=False)
                pe.matmul(dst, whi, mlo, start=False, stop=False)
                return pe.matmul(dst, wlo, mhi, start=False, stop=stop)

            def mod_vector(v, p_):
                pe.wait_ge(s_adaA, KD * (v + 1))
                for d in range(KD):
                    last = pe.matmul(ps[:, p_, 0, d:d + 1], ada_acc[:, d * P:(d + 1) * P], ones[:, 0:1],
                                     start=True, stop=True)
                last.then_inc(s_adaP, 1)
                pe.wait_ge(s_mod, v + 1)

            def norm_sum(nm, first_wait=None):
                pe.wait_ge(nm.added, KD)
                for hf in range(HALVES):
                    last = pe.matmul(ps[:, 0, hf], ones[:, :], sq_sum[:, hf * BANK:(hf + 1) * BANK],
                                     start=True, stop=True)
                last.then_inc(nm.summed, 1)

            def ffn_up(f, g, s):
                ch = 2 * g + s
                u = f.unit0 + 2 * ch
                pe.wait_ge(s_unitLo, u + 2)
                if not (isinstance(g, int) and g == 0):
                    pe.wait_ge(f.act, ch - 1)
                if not (isinstance(g, int) and g < 2):
                    pe.wait_ge(f.x, KD * (g - 2) + 6 + 2 * s)
                for k in range(KD):
                    if isinstance(g, int) and g == 0 and s == 0:
                        pe.wait_ge(f.norm.h, k + 1)
                    for i in range(2):
                        for hf in range(HALVES):
                            t = slice(hf * BANK, (hf + 1) * BANK)
                            last = three_pass(ps[:, 2 * s + i, hf], w_hi[2 * s + i][:, k], w_lo[2 * s + i][:, k],
                                              h_hi[:, k, t], h_lo[:, k, t], k == 0, k == KD - 1)
                last.then_inc(f.up, 1)
                return last

            def ffn_down(f, g, parity, last_group):
                pe.wait_ge(f.w2_lo, 2 * g + 2)
                pe.wait_ge(f.act_lo, 2 * g + 2)
                for d in range(KD):
                    p_ = d % 4
                    if d >= 4:
                        pe.wait_ge(f.x, KD * g + d - 3)
                    elif last_group:
                        pe.wait_ge(f.x, KD * (g - 1) + 5 + d)
                    else:
                        pe.wait_ge(f.act, 2 * (g + 1) + 1 + d // 2)
                    for hf in range(HALVES):
                        t = slice(hf * BANK, (hf + 1) * BANK)
                        for s in range(2):
                            last = three_pass(ps[:, p_, hf], w2_hi[:, s, d * P:(d + 1) * P],
                                              w2_lo[:, s, d * P:(d + 1) * P], act_hi[parity][:, s, t],
                                              act_lo[parity][:, s, t], s == 0, s == 1)
                    last.then_inc(f.down, 1)

            def ffn(f):
                def group(g, parity, ada_on):
                    peeled = isinstance(g, int)
                    if ada_on and not (peeled and g == 0):
                        group_mod(g)
                    ffn_up(f, g, 0)
                    if f.has_ada and peeled and g == 0:
                        mod_vector(ADA_FIRST - 1, 2)
                    ffn_up(f, g, 1)
                    if not (peeled and g == 0):
                        ffn_down(f, g - 1, 1 - parity, False)
                    if peeled and g == GROUPS - 1:
                        ffn_down(f, g, parity, True)

                def group_mod(g):
                    pe.wait_ge(f.act, 2 * g - 1)
                    if not (isinstance(g, int) and g < 2):
                        pe.wait_ge(f.x, KD * (g - 2) + 6)
                    mod_vector(g + ADA_FIRST - 1, 0)
                group_segments(pe, f, group, group_mod)

            def triples(n, slot, p_, t0, t1, free, h_wait=False):
                if t0 == 0:
                    pe.wait_ge(s_unitLo, U_MIX + n + 1)
                for t in range(t0, t1):
                    hf, k = t // KD, t % KD
                    if k == 0:
                        free(hf)
                    if h_wait and hf == 0:
                        pe.wait_ge(norms[1].h, k + 1)
                    cs = slice(hf * BANK, (hf + 1) * BANK)
                    last = three_pass(ps[:, p_, hf], w_hi[slot][:, k], w_lo[slot][:, k],
                                      h_hi[:, k, cs], h_lo[:, k, cs], k == 0, k == KD - 1)
                    if k == KD - 1:
                        last.then_inc(m_half, 1)

            def scores(i, n):
                e, j = n // TT, n % TT
                r, qt = slice(HD * e, HD * e + HD), slice(j * P, (j + 1) * P)
                L = (j + 1) * P
                if n == 0:
                    pe.wait_ge(a_lo, 2 * i + 2)
                    pe.wait_ge(aug_loaded, 32 * (i + 1))
                    pe.wait_ge(g_ot, i + 1)
                else:
                    pe.wait_ge(t_exp, 2 * TT * i + n)
                for hb in range((L + BANK - 1) // BANK):
                    c0, c1 = hb * BANK, min(L, (hb + 1) * BANK)
                    dst = ps[:, 2, hb, 0:c1 - c0]
                    pe.matmul(dst, q_hi[r, qt], k_hi[r, c0:c1], start=True, stop=False)
                    pe.matmul(dst, q_hi[r, qt], k_lo[r, c0:c1], start=False, stop=False)
                    pe.matmul(dst, q_lo[r, qt], k_hi[r, c0:c1], start=False, stop=False)
                    if c1 == L:
                        pe.matmul(ps[:, 2, hb, L - P - c0:L - c0], ident_bf[:, :], causal_bf[:, :], start=False, stop=False)
                    last = pe.matmul(dst, aug[64 * e:64 * e + 4, 0, qt], aug[64 * e:64 * e + 4, 1, c0:c1],
                                     start=False, stop=True)
                last.then_inc(t_S, 1)

            def turn_probs(i, n):
                j = n % TT
                pe.wait_ge(t_P, 2 * TT * i + n + 1)
                if n == 0:
                    pe.wait_ge(m_copied, 2 + 10 * i)
                else:
                    pe.wait_ge(t_lo, 2 * TT * i + n)
                for kb in range(j + 1):
                    last = pe.transpose(ps[:, 1, kb // 4, (kb % 4) * P:(kb % 4 + 1) * P],
                                        probs[:, n % 2, kb * P:(kb + 1) * P], ident[:, :])
                last.then_inc(t_T, 1)

            def pv(i, n):
                j = n % TT
                if n == 0:
                    pe.wait_ge(a_vlo, i + 1)
                pe.wait_ge(t_lo, 2 * TT * i + n + 1)
                if n >= 2:
                    pe.wait_ge(t_O, 2 * TT * i + n - 1)
                for kb in range(j + 1):
                    last = three_pass(ps[:, 3, n % 2, 0:P], v_hi[:, kb], v_lo[:, kb], pT_hi[:, kb], pT_lo[:, kb],
                                      kb == 0, kb == j)
                last.then_inc(t_PV, 1)

            def attention(i):
                n0 = 4 + PER_I * i
                free = [lambda hf: pe.wait_ge(a_n, 2 * i + 2),
                        lambda hf: pe.wait_ge(m_copied, 2 + 10 * i + 1 + hf),
                        lambda hf: pe.wait_ge(m_copied, 2 + 10 * i + 3 + hf)]
                for n in range(2 * TT + 2):
                    if n < 2 * TT:
                        scores(i, n)
                        for t in range(3 * n, 3 * n + 3):
                            unit = t // 16
                            triples(n0 + unit, unit % 2, 0, t % 16, t % 16 + 1, free[unit])
                    if n >= 2:
                        pv(i, n - 2)
                    if 1 <= n <= 2 * TT:
                        turn_probs(i, n - 1)

            def fp32_sum(dst_pair, weights, src, s):
                for hf in range(HALVES):
                    last = pe.matmul(ps[:, dst_pair, hf], weights[:, :], src[:, hf * BANK:(hf + 1) * BANK],
                                     start=True, stop=True)
                last.then_inc(s, 1)

            def turn(src, s):
                for t in range(TT):
                    last = pe.transpose(pair(3)[:, t * P:(t + 1) * P], src[:, t * P:(t + 1) * P], ident[:, :])
                last.then_inc(s, 1)

            def level(i, l):
                pe.wait_ge(l_mul, 7 * i + l + 1)
                if l >= 2:
                    pe.wait_ge(l_cp, 7 * i + l - 1)
                for t in range(TT):
                    last = pe.matmul(ps[:, 2, l % 2, t * 64:(t + 1) * 64], dec[:, (l + 1) % 2, t * P:(t + 1) * P],
                                     q_up[:, t * 64:(t + 1) * 64], start=True, stop=True)
                last.then_inc(l_P if l < 6 else l_last, 1)

            def v_turn(a):
                pe.wait_ge(m_copied, 2 + 10 * a)
                pe.wait_ge(a_ln, 2 * a + 2)
                turn(stage, a_vT)

            def hgrn(i, last_round):
                n0 = 4 + PER_I * i
                unit_i = lambda t0, t1: triples(n0 + 3, 1, 0, t0, t1, lambda hf: pe.wait_ge(m_copied, 2 + 10 * i + 5 + hf))

                def unit_q(t0, t1):
                    if not last_round:
                        triples(n0 + 4, 0, 1, t0, t1, lambda hf: pe.wait_ge(t_lo, 2 * TT * (i + 1)))

                def unit_k(t0, t1):
                    if not last_round:
                        triples(n0 + 5, 1, 0, t0, t1, lambda hf: pe.wait_ge(m_copied, 2 + 10 * i + 7 + hf))

                def unit_v(t0, t1):
                    if not last_round:
                        triples(n0 + 6, 0, 1, t0, t1, lambda hf: pe.wait_ge(a_n, 2 * i + 3))
                unit_i(0, 16)
                pe.wait_ge(g_kdT, i + 1)
                pe.wait_ge(t_O, 2 * TT * (i + 1))
                turn(dec[:, 0], g_kdP)
                unit_q(0, 8)
                pe.wait_ge(m_copied, 2 + 10 * i + 8)
                pe.wait_ge(g_kd, i + 1)
                turn(stage, g_iT)
                level(i, 0)
                unit_q(8, 16)
                pe.wait_ge(g_v, i + 1)
                for t in range(TT):
                    last = pe.matmul(pair(3)[:, t * P:(t + 1) * P], kk[:, t * P:(t + 1) * P], qh[:, t * P:(t + 1) * P],
                                     start=True, stop=True)
                last.then_inc(g_diag, 1)
                level(i, 1)
                if last_round:
                    pe.wait_ge(n_add, PAIRS)
                    fp32_sum(1, ones, osq_sum, n_sum)
                unit_k(0, 8)
                pe.wait_ge(g_diagC, i + 1)
                for t in range(TT - 1):
                    last = pe.matmul(pair(3)[:, t * P:(t + 1) * P], kd[:, t], v_tok[:, t], start=True, stop=True)
                last.then_inc(g_dS, 1)
                level(i, 2)
                if not last_round:
                    pe.wait_ge(g_state, 7 * (i + 1))
                    qk_sum_next(i, 0)
                unit_k(8, 16)
                level(i, 3)
                unit_v(0, 8)
                level(i, 4)
                if not last_round:
                    qk_sum_next(i, 1)
                unit_v(8, 16)
                level(i, 5)
                if not last_round:
                    v_turn(i + 1)
                level(i, 6)
                pe.wait_ge(g_state, 7 * (i + 1))
                pe.wait_ge(l_cp, 7 * (i + 1))
                for t in range(TT):
                    dst = pair(2)[:, t * P:(t + 1) * P]
                    last = pe.matmul(dst, v_tok[:, t], A[:, t], start=True, stop=t == 0)
                    if t:
                        last = pe.matmul(dst, state[:, t], qb[:, t * P:(t + 1) * P], start=False, stop=True)
                last.then_inc(g_o, 1)
                pe.wait_ge(g_osq, i + 1)
                if not last_round:
                    pe.wait_ge(a_vlo, i + 2)
                fp32_sum(3, ones, stage, g_osum)

            def qk_sum_next(i, n):
                pe.wait_ge(a_sq, 2 * i + 3 + n)
                if n:
                    pe.wait_ge(a_ln, 2 * i + 3)
                fp32_sum(3, block_ones, stage, a_sum)

            def mixer_pe():
                triples(0, 1, 1, 0, 16, lambda hf: None, h_wait=True)
                triples(1, 0, 1, 0, 16, lambda hf: pe.wait_ge(fg_s, 1))
                pe.wait_ge(a_sq, 1)
                fp32_sum(3, block_ones, stage, a_sum)
                triples(2, 1, 0, 0, 16, lambda hf: None)
                pe.wait_ge(a_sq, 2)
                fp32_sum(3, block_ones, stage, a_sum)
                triples(3, 0, 1, 0, 16, lambda hf: pe.wait_ge(a_n, 1))
                v_turn(0)
                with pe.Fori(0, NG - 1) as i:
                    attention(i)
                    hgrn(i, False)
                attention(NG - 1)
                hgrn(NG - 1, True)
                for d in range(KD):
                    pe.wait_ge(s_unitLo, U_MIX + N_MIX_IN + d + 1)
                    if d >= 4:
                        pe.wait_ge(p_x, d - 3)
                    for k in range(KD):
                        if d == 0:
                            pe.wait_ge(m_lo, k + 1)
                        for hf in range(HALVES):
                            cs = slice(hf * BANK, (hf + 1) * BANK)
                            last = three_pass(ps[:, d % 4, hf], w_hi[d % 2][:, k], w_lo[d % 2][:, k],
                                              h_hi[:, k, cs], h_lo[:, k, cs], k == 0, k == KD - 1)
                    last.then_inc(p_done, 1)

            pe.wait_ge(s_const, 2)
            pe.wait_ge(s_rows, 16 * 12)
            pe.transpose(ps[:, 0, 0, 0:N_ROWS], rows[0:N_ROWS, :], ident[0:N_ROWS, 0:N_ROWS]).then_inc(s_colsT, 1)
            pe.wait_ge(s_x, 16)
            for d in range(KD):
                p_ = 1 + d % 3
                if d >= 3:
                    pe.wait_ge(s_xT, d - 2)
                for t in range(TT):
                    last = pe.transpose(ps[:, p_].rearrange("p h f -> p (h f)")[:, t * P:(t + 1) * P],
                                        x_rows[:, t, d * P:(d + 1) * P], ident[:, :])
                last.then_inc(s_xt, 1)
            pe.wait_ge(s_cols, 1)
            norm_sum(norms[0])
            pe.wait_ge(norms[0].ln, 1)
            mod_vector(SH1, 0)
            mod_vector(SC1, 0)
            ffn(ffn1)
            norm_sum(norms[1])
            pe.wait_ge(norms[1].ln, 1)
            mixer_pe()
            norm_sum(norms[2])
            pe.wait_ge(norms[2].ln, 1)
            ffn(ffn2)
            for d in range(KD):
                pe.wait_ge(ffn2.x, KD * (GROUPS - 1) + d + 1)
                if d >= 4:
                    pe.wait_ge(s_outC, d - 3)
                else:
                    pe.wait_ge(ffn2.x, KD * (GROUPS - 1) + d + 5)
                for t in range(TT):
                    last = pe.transpose(pair(d % 4)[:, t * P:(t + 1) * P], xT[:, d, t * P:(t + 1) * P], ident[:, :])
                last.then_inc(s_outT, 1)

        @block.scalar
        def _(act):
            def chunk_hi(f, ch, s):
                for i in range(2):
                    act.wait_ge(s_unitL[i], 16 * (f.raw0[i] + ch + 1))
                    if not (isinstance(ch, int) and ch < 2):
                        act.wait_ge(f.up, ch - 1)
                    elif f is ffn2:
                        act.wait_ge(p_done, KD)
                    elif ch == 1:
                        act.wait_ge(s_const, CONSTS)
                    act.activation(w_hi[2 * s + i], raw[:, i], ACT.Copy).then_inc(s_unitHi, 1)

            def w2_hi_chunk(f, g, s):
                ch = 2 * g + s
                act.wait_ge(f.w2_loaded, 16 * (ch + 1))
                if not (isinstance(g, int) and g == 0):
                    act.wait_ge(f.down, KD * g)
                elif f.has_ada:
                    act.wait_ge(s_adaA, KD * ADA_FIRST)
                act.activation(w2_hi[:, s], raw2[:, :], ACT.Copy).then_inc(f.w2_hi, 1)

            def gate_chunk(f, g, s, parity):
                ch = 2 * g + s
                act.wait_ge(f.up, ch + 1)
                if not (isinstance(ch, int) and ch == 0):
                    act.wait_ge(f.act_lo, ch)
                act.activation(gated[:, :], pair(2 * s), ACT.Silu).then_inc(f.silu, 1)
                act.wait_ge(f.act, ch + 1)
                if not (isinstance(g, int) and g < 2):
                    act.wait_ge(f.down, KD * (g - 1))
                act.activation(act_hi[parity][:, s], gated[:, :], ACT.Copy).then_inc(f.act_hi, 1)

            def square(nm, d, x_sem, x0):
                act.wait_ge(x_sem, x0 + d + 1)
                if d >= 2:
                    act.wait_ge(nm.added, d - 1)
                act.activation(sq[:, d % 2], xT[:, d], ACT.Square).then_inc(nm.sq, 1)

            def norm(nm, x_sem, x0, shift, d0=0):
                for d in range(d0, KD):
                    square(nm, d, x_sem, x0)
                act.wait_ge(nm.summed, 1)
                act.activation(rstd[:, :], pair(0), ACT.Ln, bias=eps_col[:, 0:1], scale=1.0 / D).then_inc(nm.ln, 1)
                act.wait_ge(nm.ln, 1)
                act.activation(rstd[:, :], rstd[:, :], ACT.Exp, scale=-0.5).then_inc(nm.rstd, 1)
                for d in range(KD):
                    act.wait_ge(nm.t, d + 1)
                    act.activation(h_hi[:, d], sq[:, d % 2], ACT.Identity,
                                   bias=mod[:, shift, d:d + 1]).then_inc(nm.hi, 1)

            def ffn(f):
                def group(g, parity, ada_on):
                    chunk_hi(f, 2 * g + 1, 1)
                    w2_part(f, g, 0)
                    gate_chunk(f, g, 0, parity)
                    if not (isinstance(g, int) and g == GROUPS - 1):
                        chunk_hi(f, 2 * g + 2, 0)
                    gate_chunk(f, g, 1, parity)
                def w2_part(f, g, s):
                    if isinstance(g, int) and g == 0:
                        return
                    w2_hi_chunk(f, g - 1, 0)
                    w2_hi_chunk(f, g - 1, 1)
                group_segments(act, f, group)
                w2_hi_chunk(f, GROUPS - 1, 0)
                w2_hi_chunk(f, GROUPS - 1, 1)

            def mix_hi(n, slot, loaded, free):
                act.wait_ge(s_unitL[slot], 16 * loaded)
                act.wait_ge(*free)
                act.activation(w_hi[slot], raw[:, slot], ACT.Copy).then_inc(s_unitHi, 1)

            def round_hi(i, pos):
                slot = pos % 2
                n = 4 + PER_I * i + pos
                mix_hi(n, slot, RAW_MIX[slot] + RAW_PER_I[slot] * i + pos // 2 + 1,
                       (m_half, 2 * n if pos == 0 else 2 * n - 2))

            def exp_tile(i, n):
                j = n % TT
                L = (j + 1) * P
                act.wait_ge(t_max, 2 * TT * i + n + 1)
                if n >= 2:
                    act.wait_ge(t_T, 2 * TT * i + n - 1)
                act.activation(probs[:, n % 2, 0:L], pair(2)[:, 0:L], ACT.Exp, bias=neg_max[:, n % 2:n % 2 + 1],
                               accum_out=row_sum[:, n % 2:n % 2 + 1]).then_inc(t_exp, 1)

            def pT_hi_tile(i, n):
                j = n % TT
                act.wait_ge(t_T, 2 * TT * i + n + 1)
                if n:
                    act.wait_ge(t_PV, 2 * TT * i + n)
                act.activation(pT_hi[:, 0:j + 1].rearrange("p t k -> p (t k)"), pair(1)[:, 0:(j + 1) * P],
                               ACT.Copy).then_inc(t_hi, 1)

            def copy_half(dst, n, p_, hf):
                act.wait_ge(m_half, 2 * n + hf + 1)
                act.activation(dst[:, hf * BANK:(hf + 1) * BANK], ps[:, p_, hf], ACT.Copy).then_inc(m_copied, 1)

            def attention(i):
                n0 = 4 + PER_I * i
                copies = {3: (z_b, 0, 0), 6: (z_b, 0, 1), 8: (qh, 1, 0), 11: (qh, 1, 1), 14: (gh, 2, 0), 16: (gh, 2, 1)}
                for n in range(2 * TT + 2):
                    if n < 2 * TT:
                        exp_tile(i, n)
                    if 1 <= n <= 2 * TT:
                        pT_hi_tile(i, n - 1)
                    if n == 0:
                        round_hi(i, 1)
                    if n in copies:
                        dst, unit, hf = copies[n]
                        if n == 3:
                            act.wait_ge(fg_stored, 16 * 8)
                        copy_half(dst, n0 + unit, 0, hf)
                    if n == 6:
                        round_hi(i, 2)
                    if n == 11:
                        round_hi(i, 3)

            def sum_to_rstd(buf, p_, count, summed, ln, rstd_, turn_):
                act.wait_ge(summed, turn_)
                act.activation(buf[:, :], pair(p_), ACT.Ln, bias=eps_col[:, 0:1], scale=1.0 / count).then_inc(ln, 1)
                act.wait_ge(ln, turn_)
                act.activation(buf[:, :], buf[:, :], ACT.Exp, scale=-0.5).then_inc(rstd_, 1)

            def qk_norm(a, n, unit, p_, stage_free):
                c = 2 * a + n + 1
                act.wait_ge(m_half, 2 * unit + 2)
                if stage_free:
                    act.wait_ge(*stage_free)
                act.activation(stage[:, :], pair(p_), ACT.Square).then_inc(a_sq, 1)
                sum_to_rstd(stage, 3, HD, a_sum, a_ln, a_rstd, c)
                act.wait_ge(a_n, c)
                act.activation((q_hi, k_hi)[n][:, :], stage[:, :], ACT.Copy).then_inc(a_hi, 1)

            def v_part(a, unit):
                act.wait_ge(a_lo, 2 * a + 2)
                for hf in range(2):
                    copy_half(stage, unit, 1, hf)
                act.wait_ge(a_vT, a + 1)
                act.activation(v_hi[:, :, :].rearrange("p t k -> p (t k)"), pair(3), ACT.Copy).then_inc(a_vhi, 1)

            def level_exp(i, l):
                m = LEVELS[l]
                v = dec[:, (l + 1) % 2].rearrange("p (q e r) -> p q e r", e=2, r=m)
                act.wait_ge(l_sub, 7 * i + l + 1)
                act.activation(v[:, :, 0, :], v[:, :, 0, :], ACT.Exp, scale=-1.0).then_inc(l_exp, 1)
                act.activation(v[:, :, 1, :], v[:, :, 1, :], ACT.Exp).then_inc(l_exp, 1)

            def hgrn(i, last_round):
                n0 = 4 + PER_I * i
                act.wait_ge(t_PV, 2 * TT * (i + 1))
                act.wait_ge(m_copied, 2 + 10 * i + 6)
                act.activation(dec[:, 0], z_b[:, :], ACT.Sigmoid).then_inc(g_sig, 1)
                act.activation(kk[:, :], z_b[:, :], ACT.Sigmoid, scale=-1.0).then_inc(g_sig, 1)
                act.activation(dec[:, 1], qh[:, :], ACT.Sigmoid).then_inc(g_sig, 1)
                act.activation(A[:, :, :].rearrange("p t k -> p (t k)"), gh[:, :], ACT.Sigmoid).then_inc(g_sig, 1)
                if not last_round:
                    round_hi(i, 4)
                act.wait_ge(g_gates, 4 * i + 1)
                act.activation(dec[:, 0], dec[:, 0], ACT.Ln, bias=ln_floor[:, 0:1]).then_inc(g_ln, 1)
                act.wait_ge(g_kd0, i + 1)
                act.activation(dec[:, 0], dec[:, 0], ACT.Exp).then_inc(g_e, 1)
                level_exp(i, 0)
                act.activation(qb[:, :], z_b[:, :], ACT.Exp).then_inc(g_e, 1)
                act.activation(chunk_decay[:, :], z_b[:, P - 1:S:P], ACT.Exp).then_inc(g_e, 1)
                for hf in range(2):
                    copy_half(stage, n0 + 3, 0, hf)
                if not last_round:
                    round_hi(i, 5)
                act.wait_ge(g_kdP, i + 1)
                act.activation(kd[:, :, :].rearrange("p t k -> p (t k)"), pair(3), ACT.Copy).then_inc(g_kd, 1)
                level_exp(i, 1)
                act.wait_ge(g_iT, i + 1)
                act.activation(v_tok[:, :, :].rearrange("p t k -> p (t k)"), pair(3), ACT.Copy).then_inc(g_v, 1)
                if last_round:
                    for d in range(PAIRS):
                        if d >= 2:
                            act.wait_ge(n_add, d - 1)
                        act.activation(osq[:, d % 2], mixed[:, d], ACT.Square).then_inc(n_sq, 1)
                level_exp(i, 2)
                if not last_round:
                    qk_norm(i + 1, 0, n0 + 4, 1, (g_iT, i + 1))
                    round_hi(i, 6)
                else:
                    sum_to_rstd(orstd, 1, DA, n_sum, n_ln, n_rstd, 1)
                level_exp(i, 3)
                if last_round:
                    for d in range(PAIRS):
                        act.wait_ge(n_t, d + 1)
                        act.activation(h_hi[:, d], osq[:, d % 2], ACT.Copy).then_inc(m_hi, 1)
                level_exp(i, 4)
                if not last_round:
                    qk_norm(i + 1, 1, n0 + 5, 0, (a_lo, 2 * i + 3))
                else:
                    for j in range(2):
                        mix_hi(N_MIX_IN + j, j, RAW_FFN2[j] - KD // 2 + 1, (m_half, 2 * N_MIX_IN))
                level_exp(i, 5)
                if last_round:
                    for d in range(PAIRS, KD - 1):
                        act.wait_ge(g_mixed, d - PAIRS + 1)
                        act.activation(h_hi[:, d], mixed[:, d], ACT.Copy).then_inc(m_hi, 1)
                level_exp(i, 6)
                if not last_round:
                    v_part(i + 1, n0 + 6)
                    round_hi(i + 1, 0)
                act.wait_ge(g_o, i + 1)
                if not last_round:
                    act.wait_ge(a_vT, i + 2)
                act.activation(stage[:, :], pair(2), ACT.Square).then_inc(g_osq, 1)
                sum_to_rstd(stage, 3, P, g_osum, g_oln, g_orstd, i + 1)
                if last_round:
                    act.wait_ge(g_mixed, NG)
                    act.activation(h_hi[:, KD - 1], mixed[:, KD - 1], ACT.Copy).then_inc(m_hi, 1)

            def mixer_act():
                mix_hi(0, 1, CF + 1, (ffn1.up, CF))
                mix_hi(1, 0, CF + 1, (ffn1.up, CF))
                act.wait_ge(fg_s, 1)
                act.activation(fg_l[:, :], fg_t[:, :], ACT.Abs).then_inc(fg_s, 1)
                act.wait_ge(fg_s, 2)
                act.activation(fg_l[:, :], fg_l[:, :], ACT.Exp, scale=-1.0).then_inc(fg_s, 1)
                act.wait_ge(fg_s, 3)
                act.activation(fg_l[:, :], fg_l[:, :], ACT.Ln, bias=1.0).then_inc(fg_s, 1)
                act.wait_ge(fg_s, 6)
                act.activation(fg4[:, 0], fg_F[:, :], ACT.Copy).then_inc(fg_s, 1)
                act.activation(fg4[:, 2], fg_F[:, :], ACT.Copy, scale=-1.0).then_inc(fg_s, 1)
                mix_hi(2, 1, CF + 2, (m_half, 2))
                act.wait_ge(fg_s, 10)
                for e in range(2):
                    act.dma_start(f_rows[:, 0, e, :], fg4[:, e].bitcast(F32)).then_inc(fg_stored, 16)
                    act.dma_start(f_rows[:, 0, 2 + e, :], fg_one[:, :]).then_inc(fg_stored, 16)
                    act.dma_start(f_rows[:, 1, e, :], fg_one[:, :]).then_inc(fg_stored, 16)
                    act.dma_start(f_rows[:, 1, 2 + e, :], fg4[:, 2 + e].bitcast(F32)).then_inc(fg_stored, 16)
                qk_norm(0, 0, 1, 1, None)
                mix_hi(3, 0, CF + 2, (m_half, 4))
                qk_norm(0, 1, 2, 0, (a_lo, 1))
                v_part(0, 3)
                round_hi(0, 0)
                with act.Fori(0, NG - 1) as i:
                    attention(i)
                    hgrn(i, False)
                attention(NG - 1)
                hgrn(NG - 1, True)
                for d in range(2, KD):
                    mix_hi(N_MIX_IN + d, d % 2, RAW_FFN2[d % 2] - KD // 2 + d // 2 + 1, (p_done, d - 1))
                    square(norms[2], d - 2, p_x, 0)

            act.wait_ge(s_cols, 1)
            act.activation(c_silu[:, :], cols[:, ROW_C:ROW_B], ACT.Silu).then_inc(s_csilu, 1)
            act.wait_ge(s_lbe, 2)
            act.activation(lb_e[:, :, :], lb_e[:, :, :], ACT.Exp).then_inc(s_lbe, 1)
            for d in range(KD):
                act.wait_ge(s_xt, d + 1)
                act.activation(xT[:, d], pair(1 + d % 3), ACT.Copy).then_inc(s_xT, 1)
            norm(norms[0], s_xT, 0, SH1)
            chunk_hi(ffn1, 0, 0)
            ffn(ffn1)
            norm(norms[1], ffn1.x, KD * (GROUPS - 1), SHM)
            mixer_act()
            norm(norms[2], p_x, 0, SH2, d0=KD - 2)
            chunk_hi(ffn2, 0, 0)
            ffn(ffn2)
            for d in range(KD):
                act.wait_ge(s_outT, d + 1)
                if d >= 2:
                    act.wait_ge(s_outS[d % 2], 16 * (d // 2))
                act.activation(out_rows[:, d % 2], pair(d % 4).rearrange("p (t j) -> p t j", j=P), ACT.Copy).then_inc(s_outC, 1)
                act.wait_ge(s_outC, d + 1)
                act.dma_start(out[0].rearrange("(t p) d -> p t d", p=P)[:, :, d * P:(d + 1) * P],
                              out_rows[:, d % 2]).then_inc(s_outS[d % 2], 16)

        @block.vector
        def _(dve):
            def add_square(nm, d):
                dve.wait_ge(nm.sq, d + 1)
                if d == 1:
                    dve.tensor_tensor(sq_sum[:, :], sq[:, 0], sq[:, 1], ALU.add).then_inc(nm.added, 2)
                if d > 1:
                    dve.wait_ge(nm.added, d)
                    dve.tensor_tensor(sq_sum[:, :], sq_sum[:, :], sq[:, d % 2], ALU.add).then_inc(nm.added, 1)

            def norm_add(nm):
                for d in range(KD):
                    add_square(nm, d)

            def norm_apply(nm, shift):
                dve.wait_ge(nm.rstd, 1)

                def scale(d):
                    dve.scalar_tensor_tensor(sq[:, d % 2], xT[:, d], amp[:, nm.n, d:d + 1], rstd[:, :],
                                             ALU.mult, ALU.mult).then_inc(nm.t, 1)

                def lo(d):
                    dve.wait_ge(nm.hi, d + 1)
                    dve.scalar_tensor_tensor(h_lo[:, d], sq[:, d % 2], mod[:, shift, d:d + 1],
                                             h_hi[:, d].bitcast(F32), ALU.add, ALU.subtract).then_inc(nm.h, 1)
                scale(0)
                for d in range(KD):
                    if d + 1 < KD:
                        if d >= 1:
                            dve.wait_ge(nm.h, d)
                        scale(d + 1)
                    lo(d)

            def ada_add(v, k, src, loaded, turn):
                dve.wait_ge(loaded, turn)
                if k == 0:
                    if not (isinstance(v, int) and v == 0):
                        dve.wait_ge(s_adaP, v)
                    dve.tensor_scalar(ada_acc[:, :], src, c_silu[:, 0:1], None, ALU.mult).then_inc(s_adaA, 1)
                else:
                    dve.wait_ge(s_adaA, KD * v + k)
                    dve.scalar_tensor_tensor(ada_acc[:, :], src, c_silu[:, k:k + 1], ada_acc[:, :],
                                             ALU.mult, ALU.add).then_inc(s_adaA, 1)

            def ada_first_vector(v):
                for k in range(KD):
                    ada_add(v, k, ada_first[:, k, :], s_adaL0[k], 16 * (v + 1))

            def ada_vector(v):
                for k in range(KD):
                    ada_add(v, k, ada_ring[:, k % 2, :], s_adaL[k % 2], 16 * (4 * (v - ADA_FIRST) + k // 2 + 1))

            def mod_read(v, p_):
                dve.wait_ge(s_adaP, v + 1)
                b0 = ROW_B + v * KD
                dve.tensor_tensor(mod[:, v, :], ps[:, p_, 0, 0:KD], cols[:, b0:b0 + KD] if isinstance(v, int)
                                  else cols[:, ROW_B:ROW_G].rearrange("p (v d) -> p v d", v=N_MOD)[:, v, :],
                                  ALU.add).then_inc(s_mod, 1)

            def make_amp(n, sc):
                dve.wait_ge(s_mod, sc + 1)
                dve.scalar_tensor_tensor(amp[:, n, :], mod[:, sc, :], 1.0, cols[:, ROW_G + n * KD:ROW_G + (n + 1) * KD],
                                         ALU.add, ALU.mult).then_inc(s_gate, 1)

            def make_gate(n, gt, scale):
                dve.wait_ge(s_mod, gt + 1)
                dve.tensor_scalar(gate[:, n, :], mod[:, gt, :], scale, None, ALU.mult).then_inc(s_gate, 1)

            def chunk_lo(f, ch, s):
                for i in range(2):
                    dve.wait_ge(s_unitHi, f.unit0 + 2 * ch + i + 1)
                    dve.tensor_tensor(w_lo[2 * s + i], raw[:, i], w_hi[2 * s + i].bitcast(F32),
                                      ALU.subtract).then_inc(s_unitLo, 1)

            def w2_lo_chunk(f, g, s):
                dve.wait_ge(f.w2_hi, 2 * g + s + 1)
                dve.tensor_tensor(w2_lo[:, s], raw2[:, :], w2_hi[:, s].bitcast(F32), ALU.subtract).then_inc(f.w2_lo, 1)

            def gate_chunk(f, g, s, parity):
                ch = 2 * g + s
                dve.wait_ge(f.silu, ch + 1)
                dve.tensor_tensor(gated[:, :], pair(2 * s + 1), gated[:, :], ALU.mult).then_inc(f.act, 1)
                dve.wait_ge(f.act_hi, ch + 1)
                dve.tensor_tensor(act_lo[parity][:, s], gated[:, :], act_hi[parity][:, s].bitcast(F32),
                                  ALU.subtract).then_inc(f.act_lo, 1)

            def update(f, g, nm=None):
                for d in range(KD):
                    if nm and d:
                        add_square(nm, d - 1)
                    dve.wait_ge(f.down, KD * g + d + 1)
                    dve.scalar_tensor_tensor(xT[:, d], pair(d % 4), gate[:, f.gate, d:d + 1], xT[:, d],
                                             ALU.mult, ALU.add).then_inc(f.x, 1)

            def ffn(f):
                def group(g, parity, ada_on):
                    peeled = isinstance(g, int)
                    if ada_on and not (peeled and g == 0):
                        mod_read(g + ADA_FIRST - 1, 0)
                    chunk_lo(f, 2 * g + 1, 1)
                    if not (peeled and g == 0):
                        w2_lo_chunk(f, g - 1, 0)
                        w2_lo_chunk(f, g - 1, 1)
                    elif f.has_ada:
                        ada_first_vector(ADA_FIRST - 1)
                        mod_read(ADA_FIRST - 1, 2)
                        make_gate(0, GT1, 0.5)
                    gate_chunk(f, g, 0, parity)
                    if not (peeled and g == GROUPS - 1):
                        chunk_lo(f, 2 * g + 2, 0)
                    if ada_on:
                        ada_vector(g + ADA_FIRST)
                    gate_chunk(f, g, 1, parity)
                    if not (peeled and g == 0):
                        update(f, g - 1)
                group_segments(dve, f, group, lambda g: mod_read(g + ADA_FIRST - 1, 0))
                w2_lo_chunk(f, GROUPS - 1, 0)
                w2_lo_chunk(f, GROUPS - 1, 1)
                if f is ffn1:
                    make_amp(1, SCM)
                    make_gate(1, GTM, 1.0)
                    make_amp(2, SC2)
                    make_gate(2, GT2, 0.5)
                update(f, GROUPS - 1, norms[1] if f is ffn1 else None)
                if f is ffn1:
                    add_square(norms[1], KD - 1)

            def mix_lo(n, slot):
                dve.wait_ge(s_unitHi, U_MIX + n + 1)
                dve.tensor_tensor(w_lo[slot], raw[:, slot], w_hi[slot].bitcast(F32), ALU.subtract).then_inc(s_unitLo, 1)

            def round_lo(i, pos):
                mix_lo(4 + PER_I * i + pos, pos % 2)

            def row_max(i, n):
                L = (n % TT + 1) * P
                dve.wait_ge(t_S, 2 * TT * i + n + 1)
                dve.tensor_reduce(neg_max[:, n % 2:n % 2 + 1], pair(2)[:, 0:L], AX_X, ALU.max, negate=True
                                  ).then_inc(t_max, 1)

            def scale_probs(i, n):
                L = (n % TT + 1) * P
                dve.wait_ge(t_exp, 2 * TT * i + n + 1)
                dve.reciprocal(row_inv[:, n % 2:n % 2 + 1], row_sum[:, n % 2:n % 2 + 1]).then_inc(t_inv, 1)
                dve.wait_ge(t_inv, 2 * TT * i + n + 1)
                dve.tensor_scalar(probs[:, n % 2, 0:L], probs[:, n % 2, 0:L], row_inv[:, n % 2:n % 2 + 1], None,
                                  ALU.mult).then_inc(t_P, 1)

            def pT_lo_tile(i, n):
                j = n % TT
                flat = lambda t: t[:, 0:j + 1].rearrange("p t k -> p (t k)")
                dve.wait_ge(t_hi, 2 * TT * i + n + 1)
                dve.tensor_tensor(flat(pT_lo), pair(1)[:, 0:(j + 1) * P], flat(pT_hi).bitcast(F32),
                                  ALU.subtract).then_inc(t_lo, 1)

            def out_tile(i, n):
                e, j = n // TT, n % TT
                r = slice(HD * e, HD * e + HD)
                dve.wait_ge(t_PV, 2 * TT * i + n + 1)
                dve.tensor_copy(mixed[r, i, j * P:(j + 1) * P], ps[r, 3, n % 2, 0:P]).then_inc(t_O, 1)

            def attention(i):
                for n in range(2 * TT + 2):
                    if n < 2 * TT:
                        row_max(i, n)
                    if 1 <= n <= 2 * TT:
                        pT_lo_tile(i, n - 1)
                    if n < 2 * TT:
                        scale_probs(i, n)
                    if n >= 2:
                        out_tile(i, n - 2)
                    if n == 0:
                        round_lo(i, 1)
                    if n == 6:
                        round_lo(i, 2)
                    if n == 11:
                        round_lo(i, 3)

            def qk_norm(a, n, p_):
                c = 2 * a + n + 1
                dve.wait_ge(a_rstd, c)
                dve.scalar_tensor_tensor(stage[:, :], pair(p_), q_gain[:, n:n + 1], stage[:, :], ALU.mult, ALU.mult
                                         ).then_inc(a_n, 1)
                dve.wait_ge(a_hi, c)
                dve.tensor_tensor((q_lo, k_lo)[n][:, :], stage[:, :], (q_hi, k_hi)[n][:, :].bitcast(F32), ALU.subtract
                                  ).then_inc(a_lo, 1)

            def v_part(a):
                dve.wait_ge(a_vhi, a + 1)
                dve.tensor_tensor(v_lo[:, :, :].rearrange("p t k -> p (t k)"), pair(3),
                                  v_hi[:, :, :].rearrange("p t k -> p (t k)").bitcast(F32), ALU.subtract).then_inc(a_vlo, 1)

            def level_sub(i, l):
                m = LEVELS[l]
                if l == 1:
                    dve.wait_ge(g_kdP, i + 1)
                if l >= 2:
                    dve.wait_ge(l_P, 6 * i + l - 1)
                bv = z_b[:, :].rearrange("p (q r) -> p q r", r=2 * m)
                dve.tensor_tensor(dec[:, (l + 1) % 2].rearrange("p (q r) -> p q r", r=2 * m), bv,
                                  bv[:, :, m - 1:m].broadcast_to([P, S // (2 * m), 2 * m]), ALU.subtract
                                  ).then_inc(l_sub, 1)

            def level_mul(i, l):
                m = LEVELS[l]
                halves = lambda t: t.rearrange("p (q e r) -> p q e r", e=2, r=m)
                dv = halves(dec[:, (l + 1) % 2])
                dve.wait_ge(l_exp, 14 * i + 2 * l + 2)
                if l >= 1:
                    dve.wait_ge(l_P, 6 * i + l)
                dve.tensor_tensor(dv[:, :, 0, :], dv[:, :, 0, :], halves(kk[:, :])[:, :, 0, :], ALU.mult)
                dve.tensor_tensor(q_up[:, :].rearrange("p (q r) -> p q r", r=m), dv[:, :, 1, :],
                                  halves(qh[:, :])[:, :, 1, :], ALU.mult).then_inc(l_mul, 1)

            def level_copy(i, l):
                m = LEVELS[l]
                dve.wait_ge(*(l_P, l + 1) if l < 6 else (l_last, 1))
                dve.wait_ge(*(l_P, 6 * i + l + 1) if l < 6 else (l_last, i + 1))
                if l == 0:
                    dve.wait_ge(g_zero, i + 1)
                if l == 1:
                    dve.wait_ge(g_diagC, i + 1)
                if l >= 2:
                    dve.wait_ge(l_cp, 7 * i + l)
                nb = P // 2 // m
                dst = A[:, :, :].rearrange("p t (q e r) -> p t q e r", e=2, r=m)[:, :, :, 1, :]
                src = ps[:, 2, l % 2, :].rearrange("p (t q r) -> p t q r", t=TT, r=m)
                msk = level_u8[:, l, :].rearrange("p (o q r) -> p o q r", o=1, r=m).broadcast_to([P, TT, nb, m])
                dve.copy_predicated(dst, msk, src).then_inc(l_cp, 1)

            def hgrn(i, last_round):
                dve.wait_ge(g_sig, 4 * i + 1)
                dve.tensor_scalar(dec[:, 0], dec[:, 0], one_less_lb[:, bass.ds(i, 1)], lb[:, bass.ds(i, 1)], ALU.mult, ALU.add
                                  ).then_inc(g_gates, 1)
                dve.wait_ge(g_sig, 4 * i + 2)
                dve.tensor_scalar(kk[:, :], kk[:, :], one_less_lb[:, bass.ds(i, 1)], None, ALU.mult).then_inc(g_gates, 1)
                dve.wait_ge(g_sig, 4 * i + 3)
                dve.tensor_tensor(qh[:, :], qh[:, :], dec[:, 1], ALU.mult).then_inc(g_gates, 1)
                dve.wait_ge(g_sig, 4 * i + 4)
                dve.tensor_tensor(gh[:, :], gh[:, :], A[:, :, :].rearrange("p t k -> p (t k)"), ALU.mult
                                  ).then_inc(g_gates, 1)
                if not last_round:
                    round_lo(i, 4)
                dve.wait_ge(g_ln, i + 1)
                for t in range(TT):
                    ts = slice(t * P, (t + 1) * P)
                    last = dve.tensor_tensor_scan(z_b[:, ts], ones[:, :], dec[:, 0, ts], 0.0, ALU.mult, ALU.add)
                last.then_inc(g_b, 1)
                dve.wait_ge(g_b, i + 1)
                bv = z_b[:, :].rearrange("p (t r) -> p t r", r=P)
                dve.tensor_tensor(dec[:, 0].rearrange("p (t r) -> p t r", r=P), bv[:, :, P - 1:P].broadcast_to([P, TT, P]),
                                  bv, ALU.subtract).then_inc(g_kd0, 1)
                level_sub(i, 0)
                dve.wait_ge(g_e, 3 * i + 1)
                dve.tensor_tensor(dec[:, 0], dec[:, 0], kk[:, :], ALU.mult).then_inc(g_kdT, 1)
                level_mul(i, 0)
                dve.wait_ge(g_e, 3 * i + 2)
                dve.tensor_tensor(qb[:, :], qb[:, :], qh[:, :], ALU.mult).then_inc(g_qb, 1)
                if not last_round:
                    round_lo(i, 5)
                level_sub(i, 1)
                level_mul(i, 1)
                level_copy(i, 0)
                dve.wait_ge(l_cp, 7 * i + 1)
                level_sub(i, 2)
                dve.wait_ge(g_diag, 1)
                dve.wait_ge(g_diag, i + 1)
                dve.copy_predicated(A[:, :, :], ident_u8[:, :].rearrange("p (o k) -> p o k", o=1).broadcast_to([P, TT, P]),
                                    pair(3).rearrange("p (t k) -> p t k", k=P)).then_inc(g_diagC, 1)
                if last_round:
                    dve.wait_ge(n_sq, 2)
                    dve.tensor_tensor(osq_sum[:, :], osq[:, 0], osq[:, 1], ALU.add).then_inc(n_add, 2)
                    for d in range(2, PAIRS):
                        dve.wait_ge(n_sq, d + 1)
                        dve.wait_ge(n_add, d)
                        dve.tensor_tensor(osq_sum[:, :], osq_sum[:, :], osq[:, d % 2], ALU.add).then_inc(n_add, 1)
                level_mul(i, 2)
                level_copy(i, 1)
                dve.wait_ge(g_dS, i + 1)
                dve.wait_ge(g_e, 3 * i + 3)
                dve.tensor_copy(state[:, 1], pair(3)[:, 0:P]).then_inc(g_state, 1)
                for t in range(1, TT - 1):
                    dve.wait_ge(g_state, 7 * i + t)
                    dve.scalar_tensor_tensor(state[:, t + 1], state[:, t], chunk_decay[:, t:t + 1],
                                             pair(3)[:, t * P:(t + 1) * P], ALU.mult, ALU.add).then_inc(g_state, 1)
                if not last_round:
                    qk_norm(i + 1, 0, 1)
                    round_lo(i, 6)
                level_sub(i, 3)
                level_mul(i, 3)
                level_copy(i, 2)
                if last_round:
                    dve.wait_ge(n_rstd, 1)
                    dve.wait_ge(m_half, 2 * N_MIX_IN)
                    for d in range(PAIRS):
                        dve.scalar_tensor_tensor(osq[:, d % 2], mixed[:, d], cols[:, ROW_AG + d:ROW_AG + d + 1],
                                                 orstd[:, :], ALU.mult, ALU.mult).then_inc(n_t, 1)
                        dve.wait_ge(m_hi, d + 1)
                        dve.tensor_tensor(h_lo[:, d], osq[:, d % 2], h_hi[:, d].bitcast(F32), ALU.subtract
                                          ).then_inc(m_lo, 1)
                level_sub(i, 4)
                level_mul(i, 4)
                level_copy(i, 3)
                if not last_round:
                    qk_norm(i + 1, 1, 0)
                else:
                    for j in range(2):
                        mix_lo(N_MIX_IN + j, j)
                level_sub(i, 5)
                level_mul(i, 5)
                level_copy(i, 4)
                if last_round:
                    for d in range(PAIRS, KD - 1):
                        dve.wait_ge(m_hi, d + 1)
                        dve.tensor_tensor(h_lo[:, d], mixed[:, d], h_hi[:, d].bitcast(F32), ALU.subtract).then_inc(m_lo, 1)
                level_sub(i, 6)
                level_mul(i, 6)
                level_copy(i, 5)
                if not last_round:
                    v_part(i + 1)
                level_copy(i, 6)
                if not last_round:
                    round_lo(i + 1, 0)
                dve.wait_ge(g_orstd, i + 1)
                dve.scalar_tensor_tensor(stage[:, :], pair(2), cols[:, ROW_HG:ROW_LB][:, bass.ds(i, 1)], stage[:, :],
                                         ALU.mult, ALU.mult).then_inc(g_ot, 1)
                dve.wait_ge(g_ot, i + 2)
                dve.tensor_tensor(mixed[:, PAIRS + i], stage[:, :], gh[:, :], ALU.mult).then_inc(g_mixed, 1)
                if last_round:
                    dve.wait_ge(m_hi, KD)
                    dve.tensor_tensor(h_lo[:, KD - 1], mixed[:, KD - 1], h_hi[:, KD - 1].bitcast(F32), ALU.subtract
                                      ).then_inc(m_lo, 1)

            def mixer_dve():
                mix_lo(0, 1)
                mix_lo(1, 0)
                dve.wait_ge(m_half, 2)
                dve.wait_ge(s_small, 16)
                dve.tensor_scalar(fg_t[:, :], ps[0:NH, 1].rearrange("p h f -> p (h f)"), b_fg[:, 0:1], None, ALU.add
                                  ).then_inc(fg_s, 1)
                dve.memset(fg_one[:, :], 1.0)
                dve.wait_ge(fg_s, 4)
                dve.scalar_tensor_tensor(fg_l[:, :], fg_t[:, :], 0.0, fg_l[:, :], ALU.min, ALU.subtract).then_inc(fg_s, 1)
                dve.wait_ge(fg_s, 5)
                dve.tensor_tensor_scan(fg_F[:, :], fg_one[:, :], fg_l[:, :], 0.0, ALU.mult, ALU.add).then_inc(fg_s, 1)
                mix_lo(2, 1)
                dve.wait_ge(fg_s, 8)
                dve.tensor_tensor(fg4[:, 1], fg_F[:, :], fg4[:, 0].bitcast(F32), ALU.subtract).then_inc(fg_s, 1)
                dve.scalar_tensor_tensor(fg4[:, 3], fg_F[:, :], -1.0, fg4[:, 2].bitcast(F32), ALU.mult, ALU.subtract
                                         ).then_inc(fg_s, 1)
                dve.wait_ge(s_spill, 16)
                dve.tensor_scalar(q_gain[:, 0:1], cols[:, ROW_Q:ROW_Q + 1], HD ** -0.5, None, ALU.mult)
                dve.tensor_copy(q_gain[:, 1:2], cols[:, ROW_K:ROW_K + 1]).then_inc(g_ot, 1)
                dve.wait_ge(g_ot, 1)
                qk_norm(0, 0, 1)
                mix_lo(3, 0)
                qk_norm(0, 1, 0)
                v_part(0)
                round_lo(0, 0)
                with dve.Fori(0, NG - 1) as i:
                    attention(i)
                    hgrn(i, False)
                attention(NG - 1)
                hgrn(NG - 1, True)
                for d in range(KD):
                    if d >= 2:
                        mix_lo(N_MIX_IN + d, d % 2)
                    dve.wait_ge(p_done, d + 1)
                    dve.wait_ge(s_back[d], 16)
                    dve.scalar_tensor_tensor(xT[:, d], pair(d % 4), gate[:, 1, d:d + 1], xT[:, d], ALU.mult, ALU.add
                                             ).then_inc(p_x, 1)
                    if d >= 1:
                        add_square(norms[2], d - 1)
                add_square(norms[2], KD - 1)

            def lower_bounds():
                a, b = cols[:, ROW_LB:ROW_LB + NG], cols[:, ROW_LB + NG:ROW_LB + 2 * NG]
                dve.tensor_tensor(lb[:, :], a, b, ALU.max).then_inc(s_lbe, 1)
                dve.wait_ge(s_lbe, 1)
                dve.tensor_tensor(lb_e[:, 0, :], a, lb[:, :], ALU.subtract)
                dve.tensor_tensor(lb_e[:, 1, :], b, lb[:, :], ALU.subtract).then_inc(s_lbe, 1)
                dve.wait_ge(s_lbe, 3)
                dve.tensor_tensor(lb[:, :], lb_e[:, 0, :], lb_e[:, 1, :], ALU.add).then_inc(s_lbe, 1)
                dve.wait_ge(s_lbe, 4)
                dve.reciprocal(one_less_lb[:, :], lb[:, :]).then_inc(s_lbe, 1)
                dve.wait_ge(s_lbe, 5)
                dve.tensor_tensor(lb[:, :], lb_e[:, 0, :], one_less_lb[:, :], ALU.mult)
                dve.tensor_tensor(one_less_lb[:, :], lb_e[:, 1, :], one_less_lb[:, :], ALU.mult).then_inc(s_lbe, 1)

            dve.wait_ge(s_colsT, 1)
            dve.tensor_copy(cols[:, :], ps[:, 0, 0, 0:N_ROWS]).then_inc(s_cols, 1)
            dve.wait_ge(s_cols, 1)
            lower_bounds()
            norm_add(norms[0])
            dve.wait_ge(s_csilu, 1)
            ada_first_vector(SH1)
            mod_read(SH1, 0)
            ada_first_vector(SC1)
            mod_read(SC1, 0)
            make_amp(0, SC1)
            dve.wait_ge(s_gate, 1)
            norm_apply(norms[0], SH1)
            chunk_lo(ffn1, 0, 0)
            ffn(ffn1)
            dve.wait_ge(s_gate, 6)
            norm_apply(norms[1], SHM)
            mixer_dve()
            norm_apply(norms[2], SH2)
            chunk_lo(ffn2, 0, 0)
            ffn(ffn2)


_INS = ['x', 'c', 'w_ada', 'b_ada', 'g_norm1', 'ffn1_w_in', 'ffn1_w_out', 'g_norm_mix', 'w_in_mix', 'b_fgate',
        'q_norm_g', 'k_norm_g', 'attn_out_g', 'hgrn_lb_logits', 'hgrn_out_g', 'w_out_mix', 'g_norm2',
        'ffn2_w_in', 'ffn2_w_out']


def kernel(**inputs):
    import numpy as _np
    import concourse.bacc as _bacc
    from concourse import mybir as _mybir
    from concourse.bass_utils import run_bass_kernel_spmd as _run

    nc = _bacc.Bacc("TRN2", target_bir_lowering=False, num_devices=1)
    arrays, args = {}, []
    for name in _INS:
        a = _np.ascontiguousarray(inputs[name])
        arrays[f"in_{name}_dram"] = a
        args.append(nc.dram_tensor(f"in_{name}_dram", a.shape, _mybir.dt.from_np(a.dtype), kind="ExternalInput").ap())
    shape = inputs['x'].shape
    out = nc.dram_tensor("out_dram", shape, _mybir.dt.float32, kind="ExternalOutput").ap()
    build(nc, *args, out)
    r = _run(nc, [arrays], core_ids=[0])
    return r.results[0]["out_dram"]
```

```python
from contextlib import ExitStack

import concourse.bass as bass
from concourse import mybir

ALU = mybir.AluOpType
ACT = mybir.ActivationFunctionType
AX_X = mybir.AxisListType.X
F32 = mybir.dt.float32
F32R = mybir.dt.float32r
BF16 = mybir.dt.bfloat16
U8 = mybir.dt.uint8

P = 128
BANK = 512
EPS = 1e-6
OUT_SLOTS = 4
N_MOD = 9
SH1, SC1, GT1, SHM, SCM, GTM, SH2, SC2, GT2 = range(N_MOD)


def build(nc, x, c, w_ada, b_ada, g_norm1, ffn1_w_in, ffn1_w_out, g_norm_mix, w_in_mix, b_fgate,
          q_norm_g, k_norm_g, attn_out_g, hgrn_lb_logits, hgrn_out_g, w_out_mix, g_norm2,
          ffn2_w_in, ffn2_w_out, out):
    _, S, D = x.shape
    KD = D // P
    TT = S // P
    HALVES = S // BANK
    F = ffn1_w_out.shape[1]
    CF = F // P
    GROUPS = CF // 2
    assert CF == 2 * GROUPS and GROUPS % 2 == 1 and KD == 8 and TT == 8

    ROW_C = 0
    ROW_B = ROW_C + KD
    ROW_G = ROW_B + N_MOD * KD
    ROW_AG = ROW_G + 3 * KD
    ROW_HG = ROW_AG + 4
    ROW_LB = ROW_HG + 4
    ROW_Q = ROW_LB + 8
    ROW_K = ROW_Q + 1
    SMALL_LOADS = 13
    N_ROWS = ROW_K + 1

    DA = attn_out_g.shape[1]
    HD = q_norm_g.shape[1]
    NH = DA // HD
    PAIRS = DA // P
    NG = hgrn_out_g.shape[1] // P
    assert HD == 64 and PAIRS == NG == 4 and D == DA + NG * P
    LEVELS = [P >> (n + 1) for n in range(7)]
    MASKED = -1e30
    COL_Q, COL_K, COL_V, COL_FG = 0, DA, 2 * DA, 3 * DA
    COL_HQ = COL_FG + NH
    COL_HF, COL_HI, COL_HG = COL_HQ + NG * P, COL_HQ + 2 * NG * P, COL_HQ + 3 * NG * P

    PER_I = 7
    N_MIX_IN = 1 + 3 + PER_I * NG - 3
    U_FFN1 = 0
    U_MIX = 2 * CF
    U_FFN2 = U_MIX + N_MIX_IN + KD
    RAW_MIX = [CF + 1 + 1, CF + 1 + 1]
    RAW_PER_I = [4, 3]
    RAW_FFN2 = [RAW_MIX[k] + RAW_PER_I[k] * (NG - 1) + 2 + KD // 2 for k in range(2)]

    ctx = ExitStack()
    with ctx:
        sem = lambda name: ctx.enter_context(nc.semaphore(name))
        top = [nc.sbuf_base + (-nc.sbuf_base) % 32]

        def place(name, shape, dt=F32, at=None):
            n = {U8: 1, BF16: 2}.get(dt, 4)
            for k in shape[1:]:
                n *= k
            off = top[0] if at is None else at
            if at is None:
                top[0] += n + (-n) % 32
            t = nc.alloc_sbuf_tensor_at(name, shape, dt, offset=off)
            return t, off

        xT, x_at = place("xT", [P, KD, S])
        h_hi, h_at = place("h_hi", [P, KD, S], F32R)
        h_lo, _ = place("h_lo", [P, KD, S], F32R)
        raw, _ = place("raw", [P, 2, KD, P])
        w01_hi, _ = place("w01_hi", [P, 2, KD, P], F32R)
        w01_lo, _ = place("w01_lo", [P, 2, KD, P], F32R)
        w23_hi, mix_at = place("w23_hi", [P, 2, KD, P], F32R)
        w23_lo, _ = place("w23_lo", [P, 2, KD, P], F32R)
        w_hi = [w01_hi[:, 0], w01_hi[:, 1], w23_hi[:, 0], w23_hi[:, 1]]
        w_lo = [w01_lo[:, 0], w01_lo[:, 1], w23_lo[:, 0], w23_lo[:, 1]]
        raw2, _ = place("raw2", [P, D])
        w2_hi, w2_at = place("w2_hi", [P, 2, D], F32R)
        w2_lo, _ = place("w2_lo", [P, 2, D], F32R)
        act_hi0, _ = place("act_hi0", [P, 2, S], F32R)
        act_lo0, _ = place("act_lo0", [P, 2, S], F32R)
        act_hi1, act1_at = place("act_hi1", [P, 2, S], F32R)
        act_lo1, _ = place("act_lo1", [P, 2, S], F32R)
        act_hi, act_lo = [act_hi0, act_hi1], [act_lo0, act_lo1]
        gated, _ = place("gated", [P, S])
        ada_ring, ring_at = place("ada_ring", [P, 2, D])
        ada_acc, _ = place("ada_acc", [P, D])
        ada_end = top[0]
        ident, _ = place("ident", [P, P])
        ones, _ = place("ones", [P, P])
        cols, _ = place("cols", [P, N_ROWS])
        c_silu, _ = place("c_silu", [P, KD])
        mod, _ = place("mod", [P, N_MOD, KD])
        amp, _ = place("amp", [P, 3, KD])
        gate, _ = place("gate", [P, 3, KD])
        eps_col, _ = place("eps_col", [P, 1])
        ln_floor, _ = place("ln_floor", [P, 1])
        block_ones, _ = place("block_ones", [P, P])
        ident_bf, _ = place("ident_bf", [P, P], BF16)
        causal_bf, _ = place("causal_bf", [P, P], BF16)
        ident_u8, _ = place("ident_u8", [P, P], U8)
        level_u8, _ = place("level_u8", [P, len(LEVELS), P // 2], U8)
        lb, _ = place("lb", [P, NG])
        one_less_lb, _ = place("one_less_lb", [P, NG])
        lb_e, _ = place("lb_e", [P, 2, NG])
        q_gain, _ = place("q_gain", [P, 2])
        b_fg, _ = place("b_fg", [NH, 1])
        rms, _ = place("rms", [P, 2 * TT])
        assert top[0] <= nc.sbuf_usable_end, (top[0], nc.sbuf_usable_end)

        K4 = 4 * S
        ov = lambda name, shape, dt, kb: place(name, shape, dt, at=mix_at + int(kb * 1024))[0]
        mixed = place("mixed", [P, KD, S], at=x_at)[0]
        q_hi, q_lo, k_hi, k_lo = [ov(n, [P, S], F32R, 4 * j) for j, n in enumerate(("q_hi", "q_lo", "k_hi", "k_lo"))]
        w_hi.append(ov("w4_hi", [P, KD, P], F32R, 16)[:, :, :])
        w_lo.append(ov("w4_lo", [P, KD, P], F32R, 20)[:, :, :])
        q_f, k_f = ov("q_f", [P, S], F32, 4), ov("k_f", [P, S], F32, 12)
        v_hi, v_lo = ov("v_hi", [P, TT, P], F32R, 16), ov("v_lo", [P, TT, P], F32R, 20)
        aug = ov("aug", [68, 2, S], F32R, 24)
        z_b, kk, qh, gh = [ov(n, [P, S], F32, 32 + 4 * j) for j, n in enumerate(("z_b", "kk", "qh", "gh"))]
        v_tok = ov("v_tok", [P, TT, P], F32, 48)
        stage = ov("stage", [P, S], F32, 52)
        probs = ov("probs", [P, 2, S], F32, 56)
        pT_hi, pT_lo = ov("pT_hi", [P, TT, P], F32R, 64), ov("pT_lo", [P, TT, P], F32R, 68)
        dec = ov("dec", [P, 2, S], F32, 56)
        q_up = ov("q_up", [P, S // 2], F32, 64)
        sig_q, f_cols, v_cols = ov("sig_q", [P, S], F32, 48), ov("f_cols", [P, S], F32, 74), ov("v_cols", [P, S], F32, 74)
        kd_cols = ov("kd_cols", [P, S], F32, 78)
        A = ov("A", [P, TT, P], F32, 66)
        qb = ov("qb", [P, S], F32, 70)
        kd = ov("kd", [P, TT, P], F32, 74)
        state = ov("state", [P, TT, P], F32, 78)
        neg_max, row_sum, row_inv = [ov(n, [P, 2], F32, 82 + j / 32) for j, n in enumerate(("neg_max", "row_sum", "row_inv"))]
        chunk_decay = ov("chunk_decay", [P, TT], F32, 83)
        fg_t, fg_l, fg_F, fg_one = [ov(n, [NH, S], F32, 68 + 4 * j) for j, n in enumerate(("fg_t", "fg_l", "fg_F", "fg_one"))]
        fg4 = ov("fg4", [NH, 4, S], F32R, 32)
        osq, osq_sum, orstd = ov("osq", [P, 2, S], F32, 16), ov("osq_sum", [P, S], F32, 24), ov("orstd", [P, S], F32, 28)
        assert mix_at + 84 * 1024 <= ada_end
        x_spill = nc.dram_tensor("x_spill", [P, KD, S], F32).ap()
        f_rows = nc.dram_tensor("f_rows", [NH, 2, 4, S], F32).ap()

        flat_unit = lambda t: t.rearrange("p k j -> p (k j)")
        w2_last_hi, w2_last_lo = lambda s: flat_unit(w_hi[2 + s]), lambda s: flat_unit(w_lo[2 + s])

        raw2_last, _ = place("raw2_last", [P, D], at=ring_at)
        x_rows, _ = place("x_rows", [P, TT, D], at=h_at)
        ada_first, _ = place("ada_first", [P, KD, D], at=w2_at)
        ada_second, _ = place("ada_second", [P, KD, D], at=h_at + 4 * KD * S)
        sq, _ = place("sq", [P, 2, S], at=act1_at)
        sq_sum, _ = place("sq_sum", [P, S], at=act1_at + 8 * S)
        rstd, _ = place("rstd", [P, S], at=act1_at + 12 * S)
        rows, _ = place("rows", [P, P], at=act1_at)
        c_low = place("c_low", [P, P], at=mix_at + 512)[0]
        c_lvl = place("c_lvl", [P, len(LEVELS), P // 2], at=mix_at + 1024)[0]
        out_rows, _ = place("out_rows", [P, OUT_SLOTS, TT, P], at=act1_at)

        ada_sum = lambda v: gated[:, :] if isinstance(v, int) and v == SC1 else ada_acc[:, :]

        ps = ctx.enter_context(nc.psum_tensor("ps", [P, 4, 2, BANK], F32))
        pair = lambda n: ps[:, n].rearrange("p h f -> p (h f)")

        s_rows = sem("rows_loaded")
        s_x = [sem(f"x_loaded{q}") for q in range(4)]
        s_const = sem("consts_built")
        s_colsT = sem("cols_transposed")
        s_cols = sem("cols_ready")
        s_csilu = sem("c_silu_ready")
        s_xt = sem("x_transposed")
        s_xT = sem("xT_copied")
        s_adaL0 = [sem(f"ada_first_loaded{k}") for k in range(KD // 2)]
        s_adaL1 = [sem(f"ada_second_loaded{k}") for k in range(KD // 2)]
        s_adaL = [sem(f"ada_loaded{k}") for k in range(2)]
        s_adaA = sem("ada_tiles_added")
        s_adaP = sem("mod_summed")
        s_mod = sem("mod_read")
        s_gate = sem("gate_ready")
        s_unitL = [sem(f"unit_loaded{k}") for k in range(2)]
        s_unitHi = sem("unit_hi_written")
        s_unitLo = sem("unit_lo_written")
        s_outT = sem("out_transposed")
        s_outC = sem("out_copied")
        s_outS = [sem(f"out_stored{k}") for k in range(OUT_SLOTS)]

        class InverseRms:
            def __init__(self, name, count, blocks, p_):
                self.count, self.blocks, self.p_ = count, blocks, p_
                self.summed = sem(name + "_squares_summed")
                self.root = sem(name + "_root")
                self.inverse = sem(name + "_inverse")
                self.spread = sem(name + "_spread")
                self.turned = sem(name + "_turned")
                self.cols = TT * blocks

        class Norm:
            def __init__(self, n):
                self.n = n
                self.sq = sem(f"norm{n}_squared")
                self.added = sem(f"norm{n}_squares_added")
                self.t = sem(f"norm{n}_scaled")
                self.hi = sem(f"norm{n}_h_hi")
                self.h = sem(f"norm{n}_h_ready")

        CONSTS = 8 + 3 * len(LEVELS)

        class Ffn:
            def __init__(self, n, unit0, raw0, norm, g, w_in, w_out, has_ada):
                self.raw0 = raw0
                self.n, self.unit0, self.norm, self.gate, self.has_ada = n, unit0, norm, g, has_ada
                self.w_in = w_in[0].rearrange("(k p) (s c j) -> p k s c j", p=P, s=2, j=P)
                self.w_out = w_out[0].rearrange("(c p) d -> c p d", p=P)
                self.w2_loaded = sem(f"ffn{n}_w2_loaded")
                self.w2_last_loaded = sem(f"ffn{n}_w2_last_loaded")
                self.w2_hi = sem(f"ffn{n}_w2_hi")
                self.w2_lo = sem(f"ffn{n}_w2_lo")
                self.up = sem(f"ffn{n}_up_done")
                self.silu = sem(f"ffn{n}_silu_done")
                self.act = sem(f"ffn{n}_gated")
                self.act_hi = sem(f"ffn{n}_act_hi")
                self.act_lo = sem(f"ffn{n}_act_lo")
                self.down = sem(f"ffn{n}_down_done")
                self.x = sem(f"ffn{n}_x_updated")

        s_spill = sem("x_spilled")
        s_back = [sem(f"x_back{d}") for d in range(KD // 2)]
        s_lbe = sem("lb_steps")
        m_half = sem("mix_half_units_done")
        m_copied = sem("mix_halves_copied")
        fg_s = sem("fg_steps")
        fg_stored = sem("f_rows_stored")
        aug_loaded = sem("aug_loaded")
        a_sq = sem("qk_squared")
        a_g = sem("qk_copied_with_gain")
        a_n = sem("qk_normed")
        a_hi = sem("qk_hi")
        a_lo = sem("qk_lo")
        a_vT = sem("v_transposed")
        a_vhi = sem("v_hi_written")
        a_vlo = sem("v_lo_written")
        t_S = sem("scores_done")
        t_max = sem("row_max_done")
        t_exp = sem("exp_done")
        t_inv = sem("row_inverse_done")
        t_P = sem("probs_scaled")
        t_T = sem("probs_transposed")
        t_hi = sem("pT_hi_written")
        t_lo = sem("pT_lo_written")
        t_PV = sem("pv_done")
        t_O = sem("attention_out_written")
        g_sig = sem("sigmoids_done")
        g_gates = sem("gates_done")
        g_ln = sem("log_f_done")
        g_b = sem("log_decays_summed")
        g_kd0 = sem("to_chunk_end")
        g_e = sem("chunk_exps_done")
        g_kdT = sem("kd_columns_ready")
        g_qb = sem("qb_ready")
        g_kdP = sem("kd_transposed")
        g_kd = sem("kd_copied")
        g_iT = sem("i_transposed")
        g_v = sem("v_tok_copied")
        g_zero = sem("A_zeroed")
        l_sub = sem("level_differences")
        l_exp = sem("level_exps")
        l_mul = sem("level_operands")
        l_P = sem("level_products")
        l_last = sem("last_level_product")
        l_cp = sem("level_copied")
        g_diag = sem("diagonal_product")
        g_diagC = sem("diagonal_copied")
        g_dS = sem("state_products")
        g_state = sem("states_ready")
        g_o = sem("hgrn_out_product")
        g_oc = sem("hgrn_out_copied_with_gain")
        g_osq = sem("hgrn_out_squared")
        g_ot = sem("hgrn_out_scaled")
        g_mixed = sem("hgrn_mixed")
        n_sq = sem("attn_out_squared")
        n_add = sem("attn_out_squares_added")
        n_t = sem("attn_out_scaled")
        m_hi = sem("mixed_hi")
        m_lo = sem("mixed_lo")
        p_done = sem("w_out_product")
        p_x = sem("mix_x_updated")
        norms = [Norm(n) for n in range(3)]
        x_rms = InverseRms("x_rms", D, 1, 3)
        qk_rms = InverseRms("qk_rms", HD, 2, 3)
        attn_rms = InverseRms("attn_out_rms", DA, 1, 3)
        hgrn_rms = InverseRms("hgrn_out_rms", P, 1, 3)
        ffn1 = Ffn(1, U_FFN1, [0, 0], norms[0], 0, ffn1_w_in, ffn1_w_out, True)
        ffn2 = Ffn(2, U_FFN2, RAW_FFN2, norms[2], 2, ffn2_w_in, ffn2_w_out, False)
        W_OUT_ORDER = [*range(PAIRS, KD - 1), *range(PAIRS), KD - 1]
        ADA_FIRST = 3

        ADDS, READS = 2, 1

        def group_segments(eng, f, body):
            first = ADDS if f.has_ada else 0
            body(0, 0, first)
            body(1, 1, first)
            with eng.Fori(1, 3 if f.has_ada else GROUPS // 2) as t:
                body(2 * t, 0, first)
                body(2 * t + 1, 1, first)
            if f.has_ada:
                body(6, 0, READS)
                body(7, 1, 0)
                with eng.Fori(4, GROUPS // 2) as t:
                    body(2 * t, 0, 0)
                    body(2 * t + 1, 1, 0)
            body(GROUPS - 1, 0, 0)

        OUT_PAIR = [3] * (KD - 2) + [(KD - 2) % 3, (KD - 1) % 3]

        def down_pair(f, g, d):
            return d % 3 if f is ffn2 and isinstance(g, int) and g == GROUPS - 1 else d % 4

        block = ctx.enter_context(nc.Block())

        @block.sync
        def _(sp):
            sp.dma_start(rows[ROW_C:ROW_B, :], c.rearrange("a (r j) -> (a r) j", j=P)).then_inc(s_rows, 16)
            sp.dma_start(rows[ROW_B:ROW_G, :], b_ada.rearrange("a (r j) -> (a r) j", j=P)).then_inc(s_rows, 16)
            for n, g in enumerate((g_norm1, g_norm_mix, g_norm2)):
                sp.dma_start(rows[ROW_G + n * KD:ROW_G + (n + 1) * KD, :],
                             g.rearrange("a (r j) -> (a r) j", j=P)).then_inc(s_rows, 16)
            sp.wait_ge(s_rows, 16 * SMALL_LOADS)
            for q in range(4):
                cq = slice(q * D // 4, (q + 1) * D // 4)
                sp.dma_start(x_rows[:, :, cq], x[0].rearrange("(t p) d -> p t d", p=P)[:, :, cq]).then_inc(s_x[q], 16)

            def load_unit(u, slot, src, behind=1):
                if not (isinstance(u, int) and u < 2):
                    sp.wait_ge(s_unitLo, u - behind)
                sp.dma_start(raw[:, slot], src).then_inc(s_unitL[slot], 16)

            def load_ffn_chunk(f, ch):
                for s in range(2):
                    load_unit(f.unit0 + 2 * ch + s, s, f.w_in[:, :, s, ch, :])

            load_ffn_chunk(ffn1, 0)
            with sp.Fori(1, CF) as ch:
                load_ffn_chunk(ffn1, ch)
            w_mix = w_in_mix[0].rearrange("(k p) n -> p k n", p=P)
            tiles = lambda c0: w_mix[:, :, c0:c0 + NG * P].rearrange("p k (i j) -> p k i j", j=P)
            tq, tk, tv, thf, thq, thg, thi = [tiles(c0) for c0 in (COL_Q, COL_K, COL_V, COL_HF, COL_HQ, COL_HG, COL_HI)]
            load_unit(U_MIX, 1, w_mix[:, :, COL_FG:COL_FG + P], behind=0)
            for n, tl in enumerate((tq, tk, tv)):
                load_unit(U_MIX + 1 + n, n % 2, tl[:, :, 0, :])
            sp.wait_ge(ffn1.x, KD * GROUPS)
            sp.dma_start(x_spill, xT[:, :, :]).then_inc(s_spill, 16)

            def load_round(i, last):
                u = U_MIX + 4 + PER_I * i
                for n, tl in enumerate((thf, thq, thg, thi)):
                    load_unit(u + n, n % 2, tl[:, :, i, :], behind=0 if n == 0 else 1)
                if not last:
                    for n, tl in enumerate((tq, tk, tv)):
                        load_unit(u + 4 + n, n % 2, tl[:, :, i + 1, :])

            with sp.Fori(0, NG - 1) as i:
                load_round(i, False)
            load_round(NG - 1, True)
            w_om = w_out_mix[0].rearrange("(k p) (d j) -> p k d j", p=P, j=P)
            for d in range(KD):
                load_unit(U_MIX + N_MIX_IN + d, d % 2, w_om[:, :, d, :])
                back = {1: [(4, 2)], 3: [(0, KD - 1), (2, KD - 1)], 5: [(6, KD)]}.get(d, [])
                for e, split in back:
                    sp.wait_ge(m_lo, split)
                    sp.dma_start(xT[:, e:e + 2], x_spill[:, e:e + 2]).then_inc(s_back[e // 2], 16)
            with sp.Fori(0, CF) as ch:
                load_ffn_chunk(ffn2, ch)
            for k in range(OUT_SLOTS):
                sp.wait_ge(s_outS[k], 16 * (KD // OUT_SLOTS))

        @block.gpsimd
        def _(pool):
            ada = w_ada[0].rearrange("(k p) (v d) -> p k v d", p=P, v=N_MOD)
            pool.memset(ident[:, :], 0.0)
            pool.memset(ones[:, :], 1.0)
            pool.memset(eps_col[:, :], EPS)
            pool.memset(ln_floor[:, :], 1e-19).then_inc(s_const, 1)
            pool.wait_ge(s_const, 1)
            pool.affine_select(out=ident[:, :], in_=ident[:, :], compare_op=ALU.not_equal, fill=1.0,
                               base=0, pattern=[[-1, P]], channel_multiplier=1).then_inc(s_const, 1)
            for v, tiles_, loaded in ((SH1, ada_first, s_adaL0), (SC1, ada_second, s_adaL1)):
                for k in range(0, KD, 2):
                    if v == SH1 and k == 2:
                        pool.wait_ge(s_rows, 16 * SMALL_LOADS)
                    if v == SC1 and k == 0:
                        pool.wait_ge(s_x[0], 16)
                    pool.dma_start(tiles_[:, k:k + 2, :], ada[:, k:k + 2, v, :]).then_inc(loaded[k // 2], 16)
            pool.memset(c_low[:, :], 0.0)
            pool.memset(c_lvl[:, :, :], 1.0).then_inc(s_const, 1)
            pool.wait_ge(s_const, 3)
            pool.memset(block_ones[:, :], 0.0).then_inc(s_const, 1)
            pool.wait_ge(s_const, 4)
            for e in range(2):
                pool.memset(block_ones[HD * e:HD * e + HD, HD * e:HD * e + HD], 1.0).then_inc(s_const, 1)
                pool.wait_ge(s_const, 5 + e)
            pool.wait_ge(s_const, 6)
            pool.affine_select(out=c_low[:, :], in_=c_low[:, :], compare_op=ALU.is_ge, fill=MASKED, base=0,
                               pattern=[[-1, P]], channel_multiplier=1).then_inc(s_const, 1)
            pool.wait_ge(s_const, 7)
            pool.tensor_copy(causal_bf[:, :], c_low[:, :])
            pool.tensor_copy(ident_bf[:, :], ident[:, :])
            pool.tensor_copy(ident_u8[:, :], ident[:, :]).then_inc(s_const, 1)
            pool.wait_ge(s_const, 8)
            for n, m in enumerate(LEVELS):
                v = c_lvl[:, n, :].rearrange("p (q r) -> p q r", r=m)
                nb = P // 2 // m
                pool.affine_select(out=v, in_=v, compare_op=ALU.is_ge, fill=0.0, base=0,
                                   pattern=[[-2 * m, nb], [0, m]], channel_multiplier=1).then_inc(s_const, 1)
                pool.wait_ge(s_const, 9 + 3 * n)
                pool.affine_select(out=v, in_=v, compare_op=ALU.is_ge, fill=0.0, base=m - 1,
                                   pattern=[[2 * m, nb], [0, m]], channel_multiplier=-1).then_inc(s_const, 1)
                pool.wait_ge(s_const, 10 + 3 * n)
                pool.tensor_copy(level_u8[:, n, :], c_lvl[:, n, :]).then_inc(s_const, 1)
                pool.wait_ge(s_const, 11 + 3 * n)
            for k in range(0, KD, 2):
                pool.wait_ge(s_adaA, k + 2)
                pool.dma_start(ada_first[:, k:k + 2, :], ada[:, k:k + 2, GT1, :]).then_inc(s_adaL0[k // 2], 16)

            def load_w2(f, ch):
                if not (isinstance(ch, int) and ch == 0):
                    pool.wait_ge(f.w2_lo, ch)
                pool.dma_start(raw2[:, :], f.w_out[ch]).then_inc(f.w2_loaded, 16)

            def load_w2_last(f):
                pool.dma_start(raw2_last[:, :], f.w_out[CF - 1]).then_inc(f.w2_last_loaded, 16)
                load_w2(f, CF - 2)

            def group(g, parity, ada_on):
                if not (isinstance(g, int) and g == 0):
                    load_w2(ffn1, 2 * g - 2)
                    load_w2(ffn1, 2 * g - 1)
                if ada_on == ADDS:
                    v = g + ADA_FIRST
                    for k in range(KD):
                        if not (isinstance(g, int) and g == 0 and k < 2):
                            pool.wait_ge(s_adaA, KD * v + k - 1)
                        pool.dma_start(ada_ring[:, k % 2, :], ada[:, k, v, :]).then_inc(s_adaL[k % 2], 16)

            group_segments(pool, ffn1, group)
            load_w2_last(ffn1)
            pool.wait_ge(fg_stored, 16 * 8)
            aug_f = aug[:, :, :].bitcast(F32)

            def load_aug(i):
                for e in range(2):
                    pool.dma_start(aug_f[64 * e:64 * e + 4], f_rows.rearrange("(i e) s r t -> i e r s t", e=2)[i, e]
                                   ).then_inc(aug_loaded, 16)
            load_aug(0)
            def clear_A(i):
                pool.wait_ge(t_PV, 2 * TT * (i + 1))
                pool.wait_ge(g_b, i + 1)
                b = z_b[:, :].rearrange("p (t k) -> p t k", k=P)
                pool.tensor_tensor(A[:, :, :], b, b, ALU.subtract).then_inc(g_zero, 1)
            clear_A(0)
            with pool.Fori(1, NG) as i:
                pool.wait_ge(t_S, 2 * TT * i)
                load_aug(i)
                clear_A(i)
            pool.wait_ge(x_rms.root, 3)
            load_w2(ffn2, 0)
            with pool.Fori(1, CF - 2) as ch:
                load_w2(ffn2, ch)
            load_w2_last(ffn2)

        @block.tensor
        def _(pe):
            def three_pass(dst, whi, wlo, mhi, mlo, start, stop):
                pe.matmul(dst, whi, mhi, start=start, stop=False)
                pe.matmul(dst, whi, mlo, start=False, stop=False)
                return pe.matmul(dst, wlo, mhi, start=False, stop=stop)

            def mod_vector(v, p_):
                pe.wait_ge(s_adaA, KD * (v + 1))
                for d in range(KD):
                    last = pe.matmul(ps[:, p_, 0, d:d + 1], ada_sum(v)[:, d * P:(d + 1) * P], ones[:, 0:1],
                                     start=True, stop=True)
                last.then_inc(s_adaP, 1)

            def token_sums(r, squares):
                for t in range(TT):
                    last = pe.matmul(pair(r.p_)[:, t * r.blocks:(t + 1) * r.blocks], squares[:, t * P:(t + 1) * P],
                                     block_ones[:, 0:P:HD] if r.blocks == 2 else ones[:, 0:1], start=True, stop=True)
                last.then_inc(r.summed, 1)

            def turn_back(r, spread, turn):
                pe.wait_ge(r.spread, turn)
                for t in range(TT):
                    last = pe.transpose(pair(r.p_)[:, t * P:(t + 1) * P], spread[:, t * P:(t + 1) * P], ident[:, :])
                last.then_inc(r.turned, 1)

            def norm_sum(nm):
                pe.wait_ge(nm.added, KD)
                token_sums(x_rms, sq_sum)

            def ffn_up(f, g, s, mod_v=None, mod_before=None):
                ch = 2 * g + s
                u = f.unit0 + 2 * ch
                pe.wait_ge(s_unitLo, u + 2)
                if not (isinstance(g, int) and g == 0):
                    pe.wait_ge(f.act, ch - 1)
                if not (isinstance(g, int) and g < 2):
                    pe.wait_ge(f.x, KD * (g - 2) + 6 + 2 * s)
                if mod_before is not None:
                    pe.wait_ge(s_mod, mod_before + 1)
                for k in range(KD):
                    if mod_v is not None and k == KD // 2:
                        if s == 1:
                            pe.wait_ge(f.act, 1)
                        elif isinstance(g, int) and g < 2:
                            pe.wait_ge(f.act, 2)
                        else:
                            pe.wait_ge(f.x, KD * (g - 2) + 7)
                        mod_vector(mod_v, 2 - 2 * s)
                    if isinstance(g, int) and g == 0 and s == 0:
                        pe.wait_ge(f.norm.h, k + 1)
                    for i in range(2):
                        for hf in range(HALVES):
                            t = slice(hf * BANK, (hf + 1) * BANK)
                            last = three_pass(ps[:, 2 * s + i, hf], w_hi[2 * s + i][:, k], w_lo[2 * s + i][:, k],
                                              h_hi[:, k, t], h_lo[:, k, t], k == 0, k == KD - 1)
                last.then_inc(f.up, 1)
                return last

            def ffn_down(f, g, parity, last_group):
                pe.wait_ge(f.w2_lo, 2 * g + 2)
                pe.wait_ge(f.act_lo, 2 * g + 2)
                store = last_group and f is ffn2
                for d in range(KD):
                    p_ = down_pair(f, g, d)
                    if store and d >= 3:
                        pe.wait_ge(f.x, KD * g + d - 2)
                    elif d >= 4:
                        pe.wait_ge(f.x, KD * g + d - 3)
                    elif last_group:
                        pe.wait_ge(f.x, KD * (g - 1) + 5 + d)
                    else:
                        pe.wait_ge(f.act, 2 * (g + 1) + 1 + d // 2)
                    for hf in range(HALVES):
                        t = slice(hf * BANK, (hf + 1) * BANK)
                        for s in range(2):
                            dd = slice(d * P, (d + 1) * P)
                            whi, wlo = (w2_last_hi(s), w2_last_lo(s)) if last_group else (w2_hi[:, s], w2_lo[:, s])
                            last = three_pass(ps[:, p_, hf], whi[:, dd], wlo[:, dd], act_hi[parity][:, s, t],
                                              act_lo[parity][:, s, t], s == 0, s == 1)
                    last.then_inc(f.down, 1)
                    if store and d >= 2:
                        turn_out(d - 2)
                if store:
                    turn_out(KD - 2)
                    turn_out(KD - 1)

            def turn_out(d):
                pe.wait_ge(ffn2.x, KD * (GROUPS - 1) + d + 1)
                if 1 <= d < KD - 2:
                    pe.wait_ge(s_outC, d)
                for t in range(TT):
                    last = pe.transpose(pair(OUT_PAIR[d])[:, t * P:(t + 1) * P], xT[:, d, t * P:(t + 1) * P], ident[:, :])
                last.then_inc(s_outT, 1)

            def ffn(f):
                def group(g, parity, ada_on):
                    peeled = isinstance(g, int)
                    if ada_on and peeled and g == 0:
                        ffn_up(f, g, 0)
                        ffn_up(f, g, 1, mod_v=GT1)
                    elif ada_on:
                        ffn_up(f, g, 0, mod_v=g + ADA_FIRST - 1, mod_before=GT1 if peeled else None)
                        ffn_up(f, g, 1, mod_before=g + ADA_FIRST - 1)
                    else:
                        ffn_up(f, g, 0)
                        ffn_up(f, g, 1)
                    if not (peeled and g == 0):
                        ffn_down(f, g - 1, 1 - parity, False)
                    if peeled and g == GROUPS - 1:
                        ffn_down(f, g, parity, True)

                group_segments(pe, f, group)

            I_BESIDE = 5

            def triples(n, slot, p_, t0, t1, free):
                if t0 == 0:
                    pe.wait_ge(s_unitLo, U_MIX + n + 1)
                for t in range(t0, t1):
                    hf, k = t // KD, t % KD
                    if k == 0:
                        free(hf)
                    cs = slice(hf * BANK, (hf + 1) * BANK)
                    last = three_pass(ps[:, p_, hf], w_hi[slot][:, k], w_lo[slot][:, k],
                                      h_hi[:, k, cs], h_lo[:, k, cs], k == 0, k == KD - 1)
                    if k == KD - 1:
                        last.then_inc(m_half, 1)

            def scores(i, n):
                e, j = n // TT, n % TT
                r, qt = slice(HD * e, HD * e + HD), slice(j * P, (j + 1) * P)
                L = (j + 1) * P
                if n == 0:
                    pe.wait_ge(a_lo, 2 * i + 2)
                    pe.wait_ge(aug_loaded, 32 * (i + 1))
                    pe.wait_ge(g_oc, i)
                else:
                    pe.wait_ge(t_exp, 2 * TT * i + n)
                for hb in range((L + BANK - 1) // BANK):
                    c0, c1 = hb * BANK, min(L, (hb + 1) * BANK)
                    dst = ps[:, 2, hb, 0:c1 - c0]
                    pe.matmul(dst, q_hi[r, qt], k_hi[r, c0:c1], start=True, stop=False)
                    pe.matmul(dst, q_hi[r, qt], k_lo[r, c0:c1], start=False, stop=False)
                    pe.matmul(dst, q_lo[r, qt], k_hi[r, c0:c1], start=False, stop=False)
                    if c1 == L:
                        pe.matmul(ps[:, 2, hb, L - P - c0:L - c0], ident_bf[:, :], causal_bf[:, :], start=False, stop=False)
                    last = pe.matmul(dst, aug[64 * e:64 * e + 4, 0, qt], aug[64 * e:64 * e + 4, 1, c0:c1],
                                     start=False, stop=True)
                last.then_inc(t_S, 1)

            def turn_probs(i, n):
                j = n % TT
                pe.wait_ge(t_P, 2 * TT * i + n + 1)
                if n == 0:
                    pe.wait_ge(a_vlo, i + 1)
                else:
                    pe.wait_ge(t_lo, 2 * TT * i + n)
                for kb in range(j + 1):
                    last = pe.transpose(ps[:, 1, kb // 4, (kb % 4) * P:(kb % 4 + 1) * P],
                                        probs[:, n % 2, kb * P:(kb + 1) * P], ident[:, :])
                last.then_inc(t_T, 1)

            def pv(i, n):
                j = n % TT
                if n == 0:
                    pe.wait_ge(a_vlo, i + 1)
                    pe.wait_ge(g_mixed, i)
                pe.wait_ge(t_lo, 2 * TT * i + n + 1)
                if n >= 2:
                    pe.wait_ge(t_O, 2 * TT * i + n - 1)
                for kb in range(j + 1):
                    last = three_pass(ps[:, 3, n % 2, 0:P], v_hi[:, kb], v_lo[:, kb], pT_hi[:, kb], pT_lo[:, kb],
                                      kb == 0, kb == j)
                last.then_inc(t_PV, 1)

            def attention(i, pending):
                n0 = 4 + PER_I * i
                free = [lambda hf: pe.wait_ge(a_g, 2 * i + 2),
                        lambda hf: pe.wait_ge(m_copied, 2 + 10 * i + 1 + hf),
                        lambda hf: pe.wait_ge(m_copied, 2 + 10 * i + 3 + hf),
                        lambda hf: pe.wait_ge(m_copied, 2 + 10 * i + 5 + hf)]
                fill = [0, 3] + [5 + 3 * n for n in range(6)] + [23 + 3*n for n in range(8)] + [46, 49, 48 + I_BESIDE]
                for n in range(2 * TT + 2):
                    if n < 2 * TT:
                        scores(i, n)
                    for t in range(fill[n], fill[n + 1]):
                        unit = t // 16
                        triples(n0 + unit, unit % 2, 0, t % 16, t % 16 + 1, free[unit])
                    if n == 0 and pending:
                        turn_back(hgrn_rms, dec[:, 1], i)
                    if n >= 2:
                        pv(i, n - 2)
                    if 1 <= n <= 2 * TT:
                        turn_probs(i, n - 1)

            def turn(src, s, p_=3):
                for t in range(TT):
                    last = pe.transpose(pair(p_)[:, t * P:(t + 1) * P], src[:, t * P:(t + 1) * P], ident[:, :])
                last.then_inc(s, 1)

            def level(i, l):
                pe.wait_ge(l_mul, 7 * i + l + 1)
                if l >= 2:
                    pe.wait_ge(l_cp, 7 * i + l - 1)
                for t in range(TT):
                    last = pe.matmul(ps[:, 2, l % 2, t * 64:(t + 1) * 64], dec[:, (l + 1) % 2, t * P:(t + 1) * P],
                                     q_up[:, t * 64:(t + 1) * 64], start=True, stop=True)
                last.then_inc(l_P if l < 6 else l_last, 1)

            def v_turn(a):
                pe.wait_ge(m_copied, 2 + 10 * a)
                turn(v_cols, a_vT, 1)

            def hgrn(i, last_round):
                n0 = 4 + PER_I * i
                unit_i = lambda t0, t1: triples(n0 + 3, 1, 0, t0, t1, lambda hf: pe.wait_ge(m_copied, 2 + 10 * i + 5 + hf))

                def unit_q(t0, t1):
                    if not last_round:
                        triples(n0 + 4, 0, 1, t0, t1, lambda hf: pe.wait_ge(t_lo, 2 * TT * (i + 1)))

                def unit_k(t0, t1):
                    if not last_round:
                        triples(n0 + 5, 1, 0, t0, t1, lambda hf: pe.wait_ge(m_copied, 2 + 10 * i + 7 + hf))

                def unit_v(t0, t1):
                    if not last_round:
                        triples(n0 + 6, 0, 1, t0, t1, lambda hf: pe.wait_ge(a_g, 2 * i + 3))
                unit_i(I_BESIDE, 8)
                pe.wait_ge(g_kdT, i + 1)
                pe.wait_ge(t_O, 2 * TT * (i + 1))
                turn(kd_cols, g_kdP)
                unit_i(8, 16)
                level(i, 0)
                unit_q(0, 8)
                pe.wait_ge(m_copied, 2 + 10 * i + 8)
                pe.wait_ge(g_kd, i + 1)
                turn(stage, g_iT)
                level(i, 1)
                unit_q(8, 16)
                pe.wait_ge(g_v, i + 1)
                for t in range(TT):
                    last = pe.matmul(pair(3)[:, t * P:(t + 1) * P], kk[:, t * P:(t + 1) * P], qh[:, t * P:(t + 1) * P],
                                     start=True, stop=True)
                last.then_inc(g_diag, 1)
                level(i, 2)
                unit_k(0, 8)
                if last_round:
                    w_out_part(0, 0, 3)
                pe.wait_ge(g_diagC, i + 1)
                for t in range(TT - 1):
                    last = pe.matmul(pair(3)[:, t * P:(t + 1) * P], kd[:, t], v_tok[:, t], start=True, stop=True)
                last.then_inc(g_dS, 1)
                level(i, 3)
                unit_k(8, 16)
                if last_round:
                    w_out_part(1, 0, 2)
                else:
                    pe.wait_ge(g_state, 7 * (i + 1))
                    qk_sum_next(i, 0)
                level(i, 4)
                if last_round:
                    w_out_part(1, 2, 3)
                unit_v(0, 8)
                if not last_round:
                    turn_back(qk_rms, stage, 2 * i + 3)
                level(i, 5)
                if last_round:
                    pe.wait_ge(g_state, 7 * NG)
                    pe.wait_ge(n_add, PAIRS)
                    token_sums(attn_rms, osq_sum)
                unit_v(8, 14)
                if not last_round:
                    qk_sum_next(i, 1)
                level(i, 6)
                unit_v(14, 16)
                if not last_round:
                    turn_back(qk_rms, stage, 2 * i + 4)
                else:
                    turn_back(attn_rms, orstd, 1)
                pe.wait_ge(g_state, 7 * (i + 1))
                pe.wait_ge(g_qb, i + 1)
                pe.wait_ge(l_cp, 7 * (i + 1))
                for t in range(TT):
                    dst = pair(2)[:, t * P:(t + 1) * P]
                    last = pe.matmul(dst, v_tok[:, t], A[:, t], start=True, stop=t == 0)
                    if t:
                        last = pe.matmul(dst, state[:, t], qb[:, t * P:(t + 1) * P], start=False, stop=True)
                last.then_inc(g_o, 1)
                if not last_round:
                    v_turn(i + 1)
                else:
                    w_out_part(0, 3, KD - 1)
                    pe.wait_ge(n_t, PAIRS)
                pe.wait_ge(g_osq, i + 1)
                if not last_round:
                    pe.wait_ge(a_n, 2 * i + 4)
                token_sums(hgrn_rms, dec[:, 1])
                if last_round:
                    w_out_part(1, 3, KD - 1)
                    turn_back(hgrn_rms, dec[:, 1], NG)
                    pe.wait_ge(g_oc, NG)
                    w_out_part(2, 0, KD - 1)

            def w_out_part(d, n0, n1):
                if n0 == 0:
                    pe.wait_ge(s_unitLo, U_MIX + N_MIX_IN + d + 1)
                for n in range(n0, n1):
                    k = W_OUT_ORDER[n]
                    if d <= 1:
                        pe.wait_ge(m_lo, n + 1)
                    for hf in range(HALVES):
                        cs = slice(hf * BANK, (hf + 1) * BANK)
                        last = three_pass(ps[:, d % 4, hf], w_hi[d % 4][:, k], w_lo[d % 4][:, k],
                                          h_hi[:, k, cs], h_lo[:, k, cs], n == 0, n == KD - 1)
                    if n == KD - 1:
                        last.then_inc(p_done, 1)

            def qk_sum_next(i, n):
                pe.wait_ge(a_sq, 2 * i + 3 + n)
                if n:
                    pe.wait_ge(a_n, 2 * i + 3)
                token_sums(qk_rms, stage)

            def mixer_pe():
                pe.wait_ge(s_unitLo, U_MIX + 2)
                for k in range(KD):
                    pe.wait_ge(norms[1].h, k + 1)
                    for p_, slot in ((0, 1), (1, 0)):
                        for hf in range(HALVES):
                            cs = slice(hf * BANK, (hf + 1) * BANK)
                            last = three_pass(ps[:, p_, hf], w_hi[slot][:, k], w_lo[slot][:, k],
                                              h_hi[:, k, cs], h_lo[:, k, cs], k == 0, k == KD - 1)
                            if k == KD - 1:
                                last.then_inc(m_half, 1)
                triples(2, 4, 0, 0, 8, lambda hf: pe.wait_ge(fg_s, 1))
                pe.wait_ge(a_sq, 1)
                token_sums(qk_rms, stage)
                triples(2, 4, 0, 8, 16, lambda hf: None)
                turn_back(qk_rms, stage, 1)
                triples(3, 1, 1, 0, 8, lambda hf: pe.wait_ge(a_g, 1))
                pe.wait_ge(a_sq, 2)
                pe.wait_ge(a_n, 1)
                token_sums(qk_rms, stage)
                triples(3, 1, 1, 8, 10, lambda hf: None)
                turn_back(qk_rms, stage, 2)
                triples(3, 1, 1, 10, 16, lambda hf: None)
                v_turn(0)
                attention(0, False)
                with pe.Fori(0, NG - 1) as i:
                    hgrn(i, False)
                    attention(i + 1, True)
                hgrn(NG - 1, True)
                for d in range(3):
                    w_out_part(d, KD - 1, KD)
                for d in range(3, KD):
                    if d == 3:
                        pe.wait_ge(g_mixed, NG)
                    else:
                        pe.wait_ge(p_x, d - 3)
                    w_out_part(d, 0, KD)

            pe.wait_ge(s_const, 2)
            pe.wait_ge(s_rows, 16 * SMALL_LOADS)
            pe.transpose(ps[:, 0, 0, 0:N_ROWS], rows[0:N_ROWS, :], ident[0:N_ROWS, 0:N_ROWS]).then_inc(s_colsT, 1)
            for d in range(KD):
                p_ = 1 + d % 3
                pe.wait_ge(s_x[d // 2], 16)
                if d >= 3:
                    pe.wait_ge(s_xT, d - 2)
                for t in range(TT):
                    last = pe.transpose(ps[:, p_].rearrange("p h f -> p (h f)")[:, t * P:(t + 1) * P],
                                        x_rows[:, t, d * P:(d + 1) * P], ident[:, :])
                last.then_inc(s_xt, 1)
            pe.wait_ge(s_cols, 1)
            pe.wait_ge(s_xT, KD - 1)
            norm_sum(norms[0])
            mod_vector(SH1, 1)
            turn_back(x_rms, rstd, 1)
            pe.wait_ge(s_mod, SH1 + 1)
            mod_vector(SC1, 1)
            pe.wait_ge(s_mod, SC1 + 1)
            ffn(ffn1)
            norm_sum(norms[1])
            turn_back(x_rms, rstd, 2)
            mixer_pe()
            norm_sum(norms[2])
            turn_back(x_rms, rstd, 3)
            ffn(ffn2)
        @block.scalar
        def _(act):
            def chunk_hi(f, ch, s):
                for i in range(2):
                    act.wait_ge(s_unitL[i], 16 * (f.raw0[i] + ch + 1))
                    if not (isinstance(ch, int) and ch < 2):
                        act.wait_ge(f.up, ch - 1)
                    elif f is ffn2:
                        act.wait_ge(p_done, KD)
                    elif ch == 1:
                        act.wait_ge(s_const, CONSTS)
                    act.activation(w_hi[2 * s + i], raw[:, i], ACT.Copy).then_inc(s_unitHi, 1)

            def w2_hi_chunk(f, g, s):
                ch = 2 * g + s
                if isinstance(g, int) and g == GROUPS - 1:
                    if s == 0:
                        act.wait_ge(f.w2_loaded, 16 * (ch + 1))
                    else:
                        act.wait_ge(f.w2_last_loaded, 16)
                    act.wait_ge(f.up, CF)
                    act.activation(w2_last_hi(s), (raw2, raw2_last)[s][:, :], ACT.Copy).then_inc(f.w2_hi, 1)
                    return
                act.wait_ge(f.w2_loaded, 16 * (ch + 1))
                if not (isinstance(g, int) and g == 0):
                    act.wait_ge(f.down, KD * g)
                elif f.has_ada:
                    act.wait_ge(s_adaA, KD * ADA_FIRST)
                act.activation(w2_hi[:, s], raw2[:, :], ACT.Copy).then_inc(f.w2_hi, 1)

            def gate_chunk(f, g, s, parity):
                ch = 2 * g + s
                act.wait_ge(f.up, ch + 1)
                if not (isinstance(ch, int) and ch == 0):
                    act.wait_ge(f.act_lo, ch)
                act.activation(gated[:, :], pair(2 * s), ACT.Silu).then_inc(f.silu, 1)
                act.wait_ge(f.act, ch + 1)
                if not (isinstance(g, int) and g < 2):
                    act.wait_ge(f.down, KD * (g - 1))
                act.activation(act_hi[parity][:, s], gated[:, :], ACT.Copy).then_inc(f.act_hi, 1)

            def square(nm, d, x_sem, x0, src=None):
                if x_sem is not None:
                    act.wait_ge(x_sem, x0 + d + 1)
                if d >= 2:
                    act.wait_ge(nm.added, d - 1)
                act.activation(sq[:, d % 2], xT[:, d] if src is None else src, ACT.Square).then_inc(nm.sq, 1)

            def rms_root(r, turn):
                act.wait_ge(r.summed, turn)
                act.activation(rms[:, 0:r.cols], pair(r.p_)[:, 0:r.cols], ACT.Sqrt, bias=eps_col[:, 0:1],
                               scale=1.0 / r.count).then_inc(r.root, 1)

            def rms_spread(r, dst, turn):
                act.wait_ge(r.inverse, turn)
                act.activation(dst[:, :].rearrange("p (c j) -> p c j", c=r.cols),
                               rms[:, 0:r.cols].rearrange("p (c o) -> p c o", o=1).broadcast_to([P, r.cols, S // r.cols]),
                               ACT.Copy).then_inc(r.spread, 1)

            def squares(nm, x_sem, x0, d0=0):
                for d in range(d0, KD):
                    square(nm, d, x_sem, x0)

            def norm_hi(nm, shift):
                rms_root(x_rms, nm.n + 1)
                rms_spread(x_rms, rstd, nm.n + 1)
                for d in range(KD):
                    act.wait_ge(nm.t, d + 1)
                    act.activation(h_hi[:, d], sq[:, d % 2], ACT.Identity,
                                   bias=mod[:, shift, d:d + 1]).then_inc(nm.hi, 1)

            def ffn(f):
                def group(g, parity, ada_on):
                    chunk_hi(f, 2 * g + 1, 1)
                    w2_part(f, g, 0)
                    gate_chunk(f, g, 0, parity)
                    if not (isinstance(g, int) and g == GROUPS - 1):
                        chunk_hi(f, 2 * g + 2, 0)
                    gate_chunk(f, g, 1, parity)
                def w2_part(f, g, s):
                    if isinstance(g, int) and g == 0:
                        return
                    w2_hi_chunk(f, g - 1, 0)
                    w2_hi_chunk(f, g - 1, 1)
                group_segments(act, f, group)
                w2_hi_chunk(f, GROUPS - 1, 0)
                w2_hi_chunk(f, GROUPS - 1, 1)

            def mix_hi(n, slot, loaded, free, w_slot=None):
                act.wait_ge(s_unitL[slot], 16 * loaded)
                act.wait_ge(*free)
                act.activation(w_hi[slot if w_slot is None else w_slot], raw[:, slot], ACT.Copy).then_inc(s_unitHi, 1)

            def round_hi(i, pos):
                slot = pos % 2
                n = 4 + PER_I * i + pos
                mix_hi(n, slot, RAW_MIX[slot] + RAW_PER_I[slot] * i + pos // 2 + 1,
                       (m_half, 2 * n if pos == 0 else 2 * n - 2))

            def exp_tile(i, n):
                j = n % TT
                L = (j + 1) * P
                act.wait_ge(t_max, 2 * TT * i + n + 1)
                if n >= 2:
                    act.wait_ge(t_T, 2 * TT * i + n - 1)
                act.activation(probs[:, n % 2, 0:L], pair(2)[:, 0:L], ACT.Exp, bias=neg_max[:, n % 2:n % 2 + 1],
                               accum_out=row_sum[:, n % 2:n % 2 + 1]).then_inc(t_exp, 1)

            def pT_hi_tile(i, n):
                j = n % TT
                act.wait_ge(t_T, 2 * TT * i + n + 1)
                if n:
                    act.wait_ge(t_PV, 2 * TT * i + n)
                act.activation(pT_hi[:, 0:j + 1].rearrange("p t k -> p (t k)"), pair(1)[:, 0:(j + 1) * P],
                               ACT.Copy).then_inc(t_hi, 1)

            def copy_half(dst, n, p_, hf):
                act.wait_ge(m_half, 2 * n + hf + 1)
                act.activation(dst[:, hf * BANK:(hf + 1) * BANK], ps[:, p_, hf], ACT.Copy).then_inc(m_copied, 1)

            def attention(i, pending):
                n0 = 4 + PER_I * i
                copies = {3: (z_b, 0, 0), 6: (z_b, 0, 1), 9: (qh, 1, 0), 11: (qh, 1, 1), 14: (gh, 2, 0), 17: (gh, 2, 1)}
                for n in range(2 * TT + 2):
                    if n < 2 * TT:
                        if n == 1 and pending:
                            act.wait_ge(hgrn_rms.turned, i)
                        exp_tile(i, n)
                    if n == 0 and pending:
                        rms_spread(hgrn_rms, dec[:, 1], i)
                    if 1 <= n <= 2 * TT:
                        pT_hi_tile(i, n - 1)
                    if n == 0:
                        round_hi(i, 1)
                    if n in copies:
                        dst, unit, hf = copies[n]
                        if n == 3:
                            act.wait_ge(fg_stored, 16 * 8)
                        copy_half(dst, n0 + unit, 0, hf)
                    if n == 6:
                        round_hi(i, 2)
                    if n == 11:
                        round_hi(i, 3)
                    if n == 8:
                        act.wait_ge(m_copied, 2 + 10 * i + 2)
                        act.activation(f_cols[:, :], z_b[:, :], ACT.Sigmoid).then_inc(g_sig, 1)
                        act.activation(kk[:, :], z_b[:, :], ACT.Sigmoid, scale=-1.0).then_inc(g_sig, 1)
                    if n == 10:
                        act.wait_ge(g_gates, 4 * i + 1)
                        act.activation(f_cols[:, :], f_cols[:, :], ACT.Ln, bias=ln_floor[:, 0:1]).then_inc(g_ln, 1)
                    if n == 14:
                        act.wait_ge(g_kd0, i + 1)
                        act.activation(kd_cols[:, :], kd_cols[:, :], ACT.Exp).then_inc(g_e, 1)
                act.wait_ge(m_copied, 2 + 10 * i + 6)
                act.activation(sig_q[:, :], qh[:, :], ACT.Sigmoid).then_inc(g_sig, 1)
                act.activation(stage[:, :], gh[:, :], ACT.Sigmoid).then_inc(g_sig, 1)

            def qk_squares(a, n, unit, p_, stage_free):
                act.wait_ge(m_half, 2 * unit + 2)
                if stage_free:
                    act.wait_ge(*stage_free)
                if isinstance(a, int) and a == n == 0:
                    act.wait_ge(g_ot, 1)
                act.activation(stage[:, :], pair(p_), ACT.Square).then_inc(a_sq, 1)
                act.activation((q_f, k_f)[n][:, :], pair(p_), ACT.Identity, scale=q_gain[:, n:n + 1]).then_inc(a_g, 1)

            def qk_root(a, n):
                rms_root(qk_rms, 2 * a + n + 1)

            def qk_spread(a, n):
                rms_spread(qk_rms, stage, 2 * a + n + 1)

            def qk_hi(a, n):
                act.wait_ge(a_n, 2 * a + n + 1)
                act.activation((q_hi, k_hi)[n][:, :], stage[:, :], ACT.Copy).then_inc(a_hi, 1)

            def v_copy(unit):
                for hf in range(2):
                    copy_half(v_cols, unit, 1, hf)

            def v_part(a):
                act.wait_ge(a_vT, a + 1)
                act.activation(v_hi[:, :, :].rearrange("p t k -> p (t k)"), pair(1), ACT.Copy).then_inc(a_vhi, 1)

            def level_exp(i, l):
                m = LEVELS[l]
                v = dec[:, (l + 1) % 2].rearrange("p (q e r) -> p q e r", e=2, r=m)
                act.wait_ge(l_sub, 7 * i + l + 1)
                act.activation(v[:, :, 0, :], v[:, :, 0, :], ACT.Exp, scale=-1.0).then_inc(l_exp, 1)
                act.activation(v[:, :, 1, :], v[:, :, 1, :], ACT.Exp).then_inc(l_exp, 1)

            def hgrn(i, last_round):
                n0 = 4 + PER_I * i
                act.wait_ge(t_PV, 2 * TT * (i + 1))
                level_exp(i, 0)
                if not last_round:
                    round_hi(i, 4)
                act.activation(qb[:, :], z_b[:, :], ACT.Exp).then_inc(g_e, 1)
                act.activation(chunk_decay[:, :], z_b[:, P - 1:S:P], ACT.Exp).then_inc(g_e, 1)
                act.wait_ge(g_kdP, i + 1)
                act.activation(kd[:, :, :].rearrange("p t k -> p (t k)"), pair(3), ACT.Copy).then_inc(g_kd, 1)
                act.wait_ge(g_gates, 4 * (i + 1))
                for hf in range(2):
                    copy_half(stage, n0 + 3, 0, hf)
                level_exp(i, 1)
                if not last_round:
                    round_hi(i, 5)
                act.wait_ge(g_iT, i + 1)
                act.activation(v_tok[:, :, :].rearrange("p t k -> p (t k)"), pair(3), ACT.Copy).then_inc(g_v, 1)
                if last_round:
                    act.wait_ge(m_half, 2 * N_MIX_IN)
                    mixed_hi(PAIRS)
                    w_out_hi(0)
                level_exp(i, 2)
                if last_round:
                    mixed_hi(PAIRS + 1)
                    mixed_hi(PAIRS + 2)
                    w_out_hi(1)
                    attn_square(0)
                    attn_square(1)
                level_exp(i, 3)
                if last_round:
                    attn_square(2)
                    attn_square(3)
                if not last_round:
                    qk_squares(i + 1, 0, n0 + 4, 1, None)
                    round_hi(i, 6)
                level_exp(i, 4)
                if not last_round:
                    qk_root(i + 1, 0)
                    qk_spread(i + 1, 0)
                level_exp(i, 5)
                if not last_round:
                    qk_hi(i + 1, 0)
                level_exp(i, 6)
                if not last_round:
                    qk_squares(i + 1, 1, n0 + 5, 0, (a_lo, 2 * i + 3))
                    qk_root(i + 1, 1)
                    qk_spread(i + 1, 1)
                    v_copy(n0 + 6)
                    round_hi(i + 1, 0)
                    qk_hi(i + 1, 1)
                else:
                    rms_root(attn_rms, 1)
                    rms_spread(attn_rms, orstd, 1)
                    w_out_hi(2)
                    w_out_hi(3)
                    for d in range(PAIRS):
                        act.wait_ge(n_t, d + 1)
                        act.activation(h_hi[:, d], osq[:, d % 2], ACT.Copy).then_inc(m_hi, 1)
                act.wait_ge(g_o, i + 1)
                act.activation(dec[:, 1], pair(2), ACT.Square).then_inc(g_osq, 1)
                if not last_round:
                    v_part(i + 1)
                act.activation(mixed[:, PAIRS + i], pair(2), ACT.Identity, scale=cols[:, ROW_HG:ROW_LB][:, bass.ds(i, 1)]
                               ).then_inc(g_oc, 1)
                rms_root(hgrn_rms, i + 1)
                if last_round:
                    rms_spread(hgrn_rms, dec[:, 1], NG)
                    act.wait_ge(g_mixed, NG)
                    act.activation(h_hi[:, KD - 1], mixed[:, KD - 1], ACT.Copy).then_inc(m_hi, 1)

            def mixed_hi(k):
                act.activation(h_hi[:, k], mixed[:, k], ACT.Copy).then_inc(m_hi, 1)

            def attn_square(d):
                if d >= 2:
                    act.wait_ge(n_add, d - 1)
                act.activation(osq[:, d % 2], mixed[:, d], ACT.Square).then_inc(n_sq, 1)

            def w_out_hi(d):
                if d < 2:
                    free = (m_half, 2 * (N_MIX_IN - 1 + d))
                elif d < 4:
                    free = (t_S, 2 * TT * NG)
                else:
                    free = (p_done, d - 3)
                mix_hi(N_MIX_IN + d, d % 2, RAW_FFN2[d % 2] - KD // 2 + d // 2 + 1, free, w_slot=d % 4)

            def mixer_act():
                mix_hi(3, 0, CF + 2, (m_half, 2), w_slot=1)
                qk_squares(0, 0, 1, 1, None)
                act.wait_ge(fg_s, 1)
                act.activation(fg_l[:, :], fg_t[:, :], ACT.Abs).then_inc(fg_s, 1)
                qk_root(0, 0)
                qk_spread(0, 0)
                act.wait_ge(fg_s, 2)
                act.activation(fg_l[:, :], fg_l[:, :], ACT.Exp, scale=-1.0).then_inc(fg_s, 1)
                act.wait_ge(fg_s, 3)
                act.activation(fg_l[:, :], fg_l[:, :], ACT.Ln, bias=1.0).then_inc(fg_s, 1)
                act.wait_ge(fg_s, 6)
                act.activation(fg4[:, 0], fg_F[:, :], ACT.Copy).then_inc(fg_s, 1)
                qk_hi(0, 0)
                act.activation(fg4[:, 2], fg_F[:, :], ACT.Copy, scale=-1.0).then_inc(fg_s, 1)
                qk_squares(0, 1, 2, 0, (a_lo, 1))
                qk_root(0, 1)
                qk_spread(0, 1)
                act.wait_ge(fg_s, 10)
                for e in range(2):
                    act.dma_start(f_rows[:, 0, e, :], fg4[:, e].bitcast(F32)).then_inc(fg_stored, 16)
                    act.dma_start(f_rows[:, 0, 2 + e, :], fg_one[:, :]).then_inc(fg_stored, 16)
                    act.dma_start(f_rows[:, 1, e, :], fg_one[:, :]).then_inc(fg_stored, 16)
                    act.dma_start(f_rows[:, 1, 2 + e, :], fg4[:, 2 + e].bitcast(F32)).then_inc(fg_stored, 16)
                mix_hi(4, 0, RAW_MIX[0] + 1, (m_half, 4))
                qk_hi(0, 1)
                v_copy(3)
                v_part(0)
                attention(0, False)
                with act.Fori(0, NG - 1) as i:
                    hgrn(i, False)
                    attention(i + 1, True)
                hgrn(NG - 1, True)
                for d in range(4, KD):
                    w_out_hi(d)
                    square(norms[2], d - 4, p_x, 0)

            act.dma_start(rows[ROW_AG:ROW_HG, :], attn_out_g.rearrange("a (r j) -> (a r) j", j=P)).then_inc(s_rows, 16)
            act.dma_start(rows[ROW_HG:ROW_LB, :], hgrn_out_g.rearrange("a (r j) -> (a r) j", j=P)).then_inc(s_rows, 16)
            act.dma_start(rows[ROW_LB:ROW_Q, :], hgrn_lb_logits.rearrange("a (r j) -> (a r) j", j=P)).then_inc(s_rows, 16)
            for r, g in ((ROW_Q, q_norm_g), (ROW_K, k_norm_g)):
                for half in range(2):
                    act.dma_start(rows[r:r + 1, 64 * half:64 * half + 64], g).then_inc(s_rows, 16)
            act.dma_start(b_fg[:, :], b_fgate.rearrange("a h -> h a")).then_inc(s_rows, 16)
            act.wait_ge(s_cols, 1)
            act.activation(c_silu[:, :], cols[:, ROW_C:ROW_B], ACT.Silu).then_inc(s_csilu, 1)
            act.wait_ge(s_lbe, 2)
            act.activation(lb_e[:, :, :], lb_e[:, :, :], ACT.Exp).then_inc(s_lbe, 1)
            for d in range(KD):
                act.wait_ge(s_xt, d + 1)
                square(norms[0], d, None, 0, pair(1 + d % 3))
                act.activation(xT[:, d], pair(1 + d % 3), ACT.Copy).then_inc(s_xT, 1)
            chunk_hi(ffn1, 0, 0)
            norm_hi(norms[0], SH1)
            ffn(ffn1)
            mix_hi(0, 1, CF + 1, (ffn1.up, CF))
            mix_hi(1, 0, CF + 1, (ffn1.up, CF))
            squares(norms[1], ffn1.x, KD * (GROUPS - 1))
            mix_hi(2, 1, CF + 2, (ffn1.down, KD * GROUPS), w_slot=4)
            norm_hi(norms[1], SHM)
            mixer_act()
            squares(norms[2], p_x, 0, d0=KD - 4)
            chunk_hi(ffn2, 0, 0)
            norm_hi(norms[2], SH2)
            ffn(ffn2)
            for d in range(KD):
                act.wait_ge(s_outT, d + 1)
                k = d % OUT_SLOTS
                if d >= OUT_SLOTS:
                    act.wait_ge(s_outS[k], 16 * (d // OUT_SLOTS))
                act.activation(out_rows[:, k], pair(OUT_PAIR[d]).rearrange("p (t j) -> p t j", j=P), ACT.Copy).then_inc(s_outC, 1)
                act.wait_ge(s_outC, d + 1)
                act.dma_start(out[0].rearrange("(t p) d -> p t d", p=P)[:, :, d * P:(d + 1) * P],
                              out_rows[:, k]).then_inc(s_outS[k], 16)

        @block.vector
        def _(dve):
            def add_square(nm, d):
                dve.wait_ge(nm.sq, d + 1)
                if d == 1:
                    dve.tensor_tensor(sq_sum[:, :], sq[:, 0], sq[:, 1], ALU.add).then_inc(nm.added, 2)
                if d > 1:
                    dve.wait_ge(nm.added, d)
                    dve.tensor_tensor(sq_sum[:, :], sq_sum[:, :], sq[:, d % 2], ALU.add).then_inc(nm.added, 1)

            def rms_inverse(r, turn):
                dve.wait_ge(r.root, turn)
                dve.reciprocal(rms[:, 0:r.cols], rms[:, 0:r.cols]).then_inc(r.inverse, 1)

            def norm_apply(nm, shift):
                dve.wait_ge(x_rms.turned, nm.n + 1)

                def scale(d):
                    dve.scalar_tensor_tensor(sq[:, d % 2], xT[:, d], amp[:, nm.n, d:d + 1], pair(x_rms.p_),
                                             ALU.mult, ALU.mult).then_inc(nm.t, 1)

                def lo(d):
                    dve.wait_ge(nm.hi, d + 1)
                    dve.scalar_tensor_tensor(h_lo[:, d], sq[:, d % 2], mod[:, shift, d:d + 1],
                                             h_hi[:, d].bitcast(F32), ALU.add, ALU.subtract).then_inc(nm.h, 1)
                scale(0)
                for d in range(KD):
                    if d + 1 < KD:
                        if d >= 1:
                            dve.wait_ge(nm.h, d)
                        scale(d + 1)
                    lo(d)

            def ada_add(v, k, src, loaded, turn):
                dve.wait_ge(loaded, turn)
                acc = ada_sum(v)
                if k == 0:
                    if not (isinstance(v, int) and v <= 1):
                        dve.wait_ge(s_adaP, v)
                    dve.tensor_scalar(acc, src, c_silu[:, 0:1], None, ALU.mult).then_inc(s_adaA, 1)
                else:
                    dve.wait_ge(s_adaA, KD * v + k)
                    dve.scalar_tensor_tensor(acc, src, c_silu[:, k:k + 1], acc, ALU.mult, ALU.add).then_inc(s_adaA, 1)

            def ada_first_add(v, k):
                if v == SC1:
                    ada_add(v, k, ada_second[:, k, :], s_adaL1[k // 2], 16)
                else:
                    ada_add(v, k, ada_first[:, k, :], s_adaL0[k // 2], 16 if v == SH1 else 32)

            def ada_vector(v, k0, k1):
                for k in range(k0, k1):
                    ada_add(v, k, ada_ring[:, k % 2, :], s_adaL[k % 2], 16 * (4 * (v - ADA_FIRST) + k // 2 + 1))

            def mod_read(v, p_):
                dve.wait_ge(s_adaP, v + 1)
                b0 = ROW_B + v * KD
                dve.tensor_tensor(mod[:, v, :], ps[:, p_, 0, 0:KD], cols[:, b0:b0 + KD] if isinstance(v, int)
                                  else cols[:, ROW_B:ROW_G].rearrange("p (v d) -> p v d", v=N_MOD)[:, v, :],
                                  ALU.add).then_inc(s_mod, 1)

            def make_amp(n, sc):
                dve.wait_ge(s_mod, sc + 1)
                dve.scalar_tensor_tensor(amp[:, n, :], mod[:, sc, :], 1.0, cols[:, ROW_G + n * KD:ROW_G + (n + 1) * KD],
                                         ALU.add, ALU.mult).then_inc(s_gate, 1)

            def make_gate(n, gt, scale):
                dve.wait_ge(s_mod, gt + 1)
                dve.tensor_scalar(gate[:, n, :], mod[:, gt, :], scale, None, ALU.mult).then_inc(s_gate, 1)

            def chunk_lo(f, ch, s):
                for i in range(2):
                    dve.wait_ge(s_unitHi, f.unit0 + 2 * ch + i + 1)
                    dve.tensor_tensor(w_lo[2 * s + i], raw[:, i], w_hi[2 * s + i].bitcast(F32),
                                      ALU.subtract).then_inc(s_unitLo, 1)

            def w2_lo_chunk(f, g, s):
                dve.wait_ge(f.w2_hi, 2 * g + s + 1)
                if isinstance(g, int) and g == GROUPS - 1:
                    dve.tensor_tensor(w2_last_lo(s), (raw2, raw2_last)[s][:, :], w2_last_hi(s).bitcast(F32), ALU.subtract
                                      ).then_inc(f.w2_lo, 1)
                else:
                    dve.tensor_tensor(w2_lo[:, s], raw2[:, :], w2_hi[:, s].bitcast(F32), ALU.subtract
                                      ).then_inc(f.w2_lo, 1)

            def gate_chunk(f, g, s, parity):
                ch = 2 * g + s
                dve.wait_ge(f.silu, ch + 1)
                dve.tensor_tensor(gated[:, :], pair(2 * s + 1), gated[:, :], ALU.mult).then_inc(f.act, 1)
                dve.wait_ge(f.act_hi, ch + 1)
                dve.tensor_tensor(act_lo[parity][:, s], gated[:, :], act_hi[parity][:, s].bitcast(F32),
                                  ALU.subtract).then_inc(f.act_lo, 1)

            def update(f, g, nm=None):
                for d in range(KD):
                    dve.wait_ge(f.down, KD * g + d + 1)
                    dve.scalar_tensor_tensor(xT[:, d], pair(down_pair(f, g, d)), gate[:, f.gate, d:d + 1], xT[:, d],
                                             ALU.mult, ALU.add).then_inc(f.x, 1)
                    if nm and d:
                        add_square(nm, d - 1)

            def ffn(f):
                def group(g, parity, ada_on):
                    peeled = isinstance(g, int)
                    chunk_lo(f, 2 * g + 1, 1)
                    if not (peeled and g == 0):
                        w2_lo_chunk(f, g - 1, 0)
                        w2_lo_chunk(f, g - 1, 1)
                    elif f.has_ada:
                        for k in range(KD):
                            ada_first_add(GT1, k)
                    if ada_on and not (peeled and g == 0):
                        mod_read(g + ADA_FIRST - 1, 2)
                    gate_chunk(f, g, 0, parity)
                    if ada_on and peeled and g == 0:
                        mod_read(GT1, 0)
                        make_gate(0, GT1, 0.5)
                    if not (peeled and g == GROUPS - 1):
                        chunk_lo(f, 2 * g + 2, 0)
                    if ada_on == ADDS:
                        ada_vector(g + ADA_FIRST, 0, 4 if peeled and g == 0 else 5)
                    gate_chunk(f, g, 1, parity)
                    if peeled and g == GROUPS - 1:
                        w2_lo_chunk(f, g, 0)
                        w2_lo_chunk(f, g, 1)
                        if f is ffn1:
                            mix_lo(0, 1)
                            mix_lo(1, 0)
                    if not (peeled and g == 0):
                        update(f, g - 1)
                    if ada_on == ADDS:
                        ada_vector(g + ADA_FIRST, 4 if peeled and g == 0 else 5, KD)
                group_segments(dve, f, group)
                if f is ffn1:
                    make_amp(1, SCM)
                    make_gate(1, GTM, 1.0)
                    make_amp(2, SC2)
                    make_gate(2, GT2, 0.5)
                update(f, GROUPS - 1, norms[1] if f is ffn1 else None)
                if f is ffn1:
                    add_square(norms[1], KD - 1)

            def mix_lo(n, slot, w_slot=None):
                w_slot = slot if w_slot is None else w_slot
                dve.wait_ge(s_unitHi, U_MIX + n + 1)
                dve.tensor_tensor(w_lo[w_slot], raw[:, slot], w_hi[w_slot].bitcast(F32), ALU.subtract).then_inc(s_unitLo, 1)

            def round_lo(i, pos):
                mix_lo(4 + PER_I * i + pos, pos % 2)

            def row_max(i, n):
                L = (n % TT + 1) * P
                dve.wait_ge(t_S, 2 * TT * i + n + 1)
                dve.tensor_reduce(neg_max[:, n % 2:n % 2 + 1], pair(2)[:, 0:L], AX_X, ALU.max, negate=True
                                  ).then_inc(t_max, 1)

            def scale_probs(i, n):
                L = (n % TT + 1) * P
                dve.wait_ge(t_exp, 2 * TT * i + n + 1)
                dve.reciprocal(row_inv[:, n % 2:n % 2 + 1], row_sum[:, n % 2:n % 2 + 1]).then_inc(t_inv, 1)
                dve.wait_ge(t_inv, 2 * TT * i + n + 1)
                dve.tensor_scalar(probs[:, n % 2, 0:L], probs[:, n % 2, 0:L], row_inv[:, n % 2:n % 2 + 1], None,
                                  ALU.mult).then_inc(t_P, 1)

            def pT_lo_tile(i, n):
                j = n % TT
                flat = lambda t: t[:, 0:j + 1].rearrange("p t k -> p (t k)")
                dve.wait_ge(t_hi, 2 * TT * i + n + 1)
                dve.tensor_tensor(flat(pT_lo), pair(1)[:, 0:(j + 1) * P], flat(pT_hi).bitcast(F32),
                                  ALU.subtract).then_inc(t_lo, 1)

            def out_tile(i, n):
                e, j = n // TT, n % TT
                r = slice(HD * e, HD * e + HD)
                dve.wait_ge(t_PV, 2 * TT * i + n + 1)
                dve.tensor_copy(mixed[r, i, j * P:(j + 1) * P], ps[r, 3, n % 2, 0:P]).then_inc(t_O, 1)

            def attention(i, pending):
                for n in range(2 * TT + 2):
                    if n < 2 * TT:
                        row_max(i, n)
                    if 1 <= n <= 2 * TT:
                        pT_lo_tile(i, n - 1)
                    if n < 2 * TT:
                        scale_probs(i, n)
                    if n == 0 and pending:
                        rms_inverse(hgrn_rms, i)
                    if n == 1 and pending:
                        mix_hgrn_out(i)
                    if n >= 2:
                        out_tile(i, n - 2)
                    if n == 0:
                        round_lo(i, 1)
                    if n == 6:
                        round_lo(i, 2)
                    if n == 11:
                        round_lo(i, 3)
                    if n == 9:
                        dve.wait_ge(g_sig, 4 * i + 1)
                        dve.tensor_scalar(f_cols[:, :], f_cols[:, :], one_less_lb[:, bass.ds(i, 1)],
                                          lb[:, bass.ds(i, 1)], ALU.mult, ALU.add).then_inc(g_gates, 1)
                        dve.wait_ge(g_sig, 4 * i + 2)
                        dve.tensor_scalar(kk[:, :], kk[:, :], one_less_lb[:, bass.ds(i, 1)], None, ALU.mult
                                          ).then_inc(g_gates, 1)
                    if n == 12:
                        dve.wait_ge(g_ln, i + 1)
                        for t in range(TT):
                            ts = slice(t * P, (t + 1) * P)
                            last = dve.tensor_tensor_scan(z_b[:, ts], ones[:, :], f_cols[:, ts], 0.0, ALU.mult, ALU.add)
                        last.then_inc(g_b, 1)
                    if n == 13:
                        dve.wait_ge(g_b, i + 1)
                        bv = z_b[:, :].rearrange("p (t r) -> p t r", r=P)
                        dve.tensor_tensor(kd_cols[:, :].rearrange("p (t r) -> p t r", r=P),
                                          bv[:, :, P - 1:P].broadcast_to([P, TT, P]), bv, ALU.subtract).then_inc(g_kd0, 1)
                    if n == 15:
                        dve.wait_ge(g_e, 3 * i + 1)
                        dve.tensor_tensor(kd_cols[:, :], kd_cols[:, :], kk[:, :], ALU.mult).then_inc(g_kdT, 1)

            def mix_hgrn_out(a):
                dve.wait_ge(g_ot, a + 1)
                dve.wait_ge(hgrn_rms.turned, a)
                tile_ = mixed[:, PAIRS - 1 + a]
                dve.tensor_tensor(tile_, tile_, pair(hgrn_rms.p_), ALU.mult).then_inc(g_mixed, 1)

            def qk_apply(a, n):
                dve.wait_ge(qk_rms.turned, 2 * a + n + 1)
                dve.tensor_tensor(stage[:, :], (q_f, k_f)[n][:, :], pair(qk_rms.p_), ALU.mult).then_inc(a_n, 1)

            def qk_lo(a, n):
                dve.wait_ge(a_hi, 2 * a + n + 1)
                dve.tensor_tensor((q_lo, k_lo)[n][:, :], stage[:, :], (q_hi, k_hi)[n][:, :].bitcast(F32), ALU.subtract
                                  ).then_inc(a_lo, 1)

            def v_part(a):
                dve.wait_ge(a_vhi, a + 1)
                dve.tensor_tensor(v_lo[:, :, :].rearrange("p t k -> p (t k)"), pair(1),
                                  v_hi[:, :, :].rearrange("p t k -> p (t k)").bitcast(F32), ALU.subtract).then_inc(a_vlo, 1)

            def level_sub(i, l):
                m = LEVELS[l]
                if l >= 2:
                    dve.wait_ge(l_P, 6 * i + l - 1)
                bv = z_b[:, :].rearrange("p (q r) -> p q r", r=2 * m)
                dve.tensor_tensor(dec[:, (l + 1) % 2].rearrange("p (q r) -> p q r", r=2 * m), bv,
                                  bv[:, :, m - 1:m].broadcast_to([P, S // (2 * m), 2 * m]), ALU.subtract
                                  ).then_inc(l_sub, 1)

            def level_mul(i, l):
                m = LEVELS[l]
                halves = lambda t: t.rearrange("p (q e r) -> p q e r", e=2, r=m)
                dv = halves(dec[:, (l + 1) % 2])
                if l == 0:
                    dve.wait_ge(g_gates, 4 * (i + 1))
                dve.wait_ge(l_exp, 14 * i + 2 * l + 2)
                if l >= 1:
                    dve.wait_ge(l_P, 6 * i + l)
                dve.tensor_tensor(dv[:, :, 0, :], dv[:, :, 0, :], halves(kk[:, :])[:, :, 0, :], ALU.mult)
                dve.tensor_tensor(q_up[:, :].rearrange("p (q r) -> p q r", r=m), dv[:, :, 1, :],
                                  halves(qh[:, :])[:, :, 1, :], ALU.mult).then_inc(l_mul, 1)

            def level_copy(i, l):
                m = LEVELS[l]
                dve.wait_ge(*(l_P, l + 1) if l < 6 else (l_last, 1))
                dve.wait_ge(*(l_P, 6 * i + l + 1) if l < 6 else (l_last, i + 1))
                if l == 1:
                    dve.wait_ge(g_diagC, i + 1)
                if l >= 2:
                    dve.wait_ge(l_cp, 7 * i + l)
                nb = P // 2 // m
                dst = A[:, :, :].rearrange("p t (q e r) -> p t q e r", e=2, r=m)[:, :, :, 1, :]
                src = ps[:, 2, l % 2, :].rearrange("p (t q r) -> p t q r", t=TT, r=m)
                msk = level_u8[:, l, :].rearrange("p (o q r) -> p o q r", o=1, r=m).broadcast_to([P, TT, nb, m])
                dve.copy_predicated(dst, msk, src).then_inc(l_cp, 1)

            def hgrn(i, last_round):
                level_sub(i, 0)
                dve.wait_ge(g_sig, 4 * i + 3)
                dve.tensor_tensor(qh[:, :], qh[:, :], sig_q[:, :], ALU.mult).then_inc(g_gates, 1)
                dve.wait_ge(g_sig, 4 * i + 4)
                dve.tensor_tensor(gh[:, :], gh[:, :], stage[:, :], ALU.mult).then_inc(g_gates, 1)
                if not last_round:
                    round_lo(i, 4)
                level_mul(i, 0)
                level_sub(i, 1)
                dve.wait_ge(g_zero, i + 1)
                dve.wait_ge(g_e, 3 * i + 2)
                dve.tensor_tensor(qb[:, :], qb[:, :], qh[:, :], ALU.mult).then_inc(g_qb, 1)
                level_mul(i, 1)
                level_copy(i, 0)
                dve.wait_ge(l_cp, 7 * i + 1)
                if not last_round:
                    round_lo(i, 5)
                level_sub(i, 2)
                if last_round:
                    mixed_lo(0)
                level_mul(i, 2)
                if last_round:
                    mix_lo(N_MIX_IN, 0)
                    mixed_lo(1)
                dve.wait_ge(g_diag, 1)
                dve.wait_ge(g_diag, i + 1)
                dve.copy_predicated(A[:, :, :], ident_u8[:, :].rearrange("p (o k) -> p o k", o=1).broadcast_to([P, TT, P]),
                                    pair(3).rearrange("p (t k) -> p t k", k=P)).then_inc(g_diagC, 1)
                level_copy(i, 1)
                level_sub(i, 3)
                if last_round:
                    mixed_lo(2)
                level_mul(i, 3)
                if last_round:
                    mix_lo(N_MIX_IN + 1, 1)
                    dve.wait_ge(n_sq, 2)
                    dve.tensor_tensor(osq_sum[:, :], osq[:, 0], osq[:, 1], ALU.add).then_inc(n_add, 2)
                    level_copy(i, 2)
                    level_sub(i, 4)
                dve.wait_ge(g_dS, i + 1)
                dve.wait_ge(g_e, 3 * i + 3)
                dve.tensor_copy(state[:, 1], pair(3)[:, 0:P]).then_inc(g_state, 1)
                for t in range(1, TT - 1):
                    dve.wait_ge(g_state, 7 * i + t)
                    dve.scalar_tensor_tensor(state[:, t + 1], state[:, t], chunk_decay[:, t:t + 1],
                                             pair(3)[:, t * P:(t + 1) * P], ALU.mult, ALU.add).then_inc(g_state, 1)
                if not last_round:
                    level_copy(i, 2)
                    round_lo(i, 6)
                    level_sub(i, 4)
                else:
                    osq_add(2)
                level_mul(i, 4)
                if not last_round:
                    rms_inverse(qk_rms, 2 * i + 3)
                level_copy(i, 3)
                level_sub(i, 5)
                if last_round:
                    osq_add(3)
                level_mul(i, 5)
                if not last_round:
                    qk_apply(i + 1, 0)
                level_copy(i, 4)
                level_sub(i, 6)
                if not last_round:
                    qk_lo(i + 1, 0)
                level_mul(i, 6)
                rms_inverse(*(attn_rms, 1) if last_round else (qk_rms, 2 * i + 4))
                level_copy(i, 5)
                level_copy(i, 6)
                if not last_round:
                    qk_apply(i + 1, 1)
                    round_lo(i + 1, 0)
                    qk_lo(i + 1, 1)
                    v_part(i + 1)
                else:
                    dve.wait_ge(attn_rms.turned, 1)
                    for d in range(PAIRS):
                        if d >= 2:
                            dve.wait_ge(m_lo, d + 2)
                        dve.scalar_tensor_tensor(osq[:, d % 2], mixed[:, d], cols[:, ROW_AG + d:ROW_AG + d + 1],
                                                 pair(attn_rms.p_), ALU.mult, ALU.mult).then_inc(n_t, 1)
                        if d >= 1:
                            attn_lo(d - 1)
                    attn_lo(PAIRS - 1)
                    for d in range(2, 4):
                        mix_lo(N_MIX_IN + d, d % 2, d)
                dve.wait_ge(g_oc, i + 1)
                dve.tensor_tensor(mixed[:, PAIRS + i], mixed[:, PAIRS + i], gh[:, :], ALU.mult).then_inc(g_ot, 1)
                if last_round:
                    rms_inverse(hgrn_rms, NG)
                    mix_hgrn_out(NG)
                    dve.wait_ge(m_hi, KD)
                    dve.tensor_tensor(h_lo[:, KD - 1], mixed[:, KD - 1], h_hi[:, KD - 1].bitcast(F32), ALU.subtract
                                      ).then_inc(m_lo, 1)

            def osq_add(d):
                dve.wait_ge(n_sq, d + 1)
                dve.wait_ge(n_add, d)
                dve.tensor_tensor(osq_sum[:, :], osq_sum[:, :], osq[:, d % 2], ALU.add).then_inc(n_add, 1)

            def mixed_lo(n):
                k = W_OUT_ORDER[n]
                dve.wait_ge(m_hi, n + 1)
                dve.tensor_tensor(h_lo[:, k], mixed[:, k], h_hi[:, k].bitcast(F32), ALU.subtract).then_inc(m_lo, 1)

            def attn_lo(d):
                dve.wait_ge(m_hi, NG + d)
                dve.tensor_tensor(h_lo[:, d], osq[:, d % 2], h_hi[:, d].bitcast(F32), ALU.subtract).then_inc(m_lo, 1)

            def mixer_dve():
                dve.tensor_scalar(q_gain[:, 0:1], cols[:, ROW_Q:ROW_Q + 1], HD ** -0.5, None, ALU.mult)
                dve.tensor_copy(q_gain[:, 1:2], cols[:, ROW_K:ROW_K + 1]).then_inc(g_ot, 1)
                mix_lo(2, 1, 4)
                dve.memset(fg_one[:, :], 1.0)
                dve.wait_ge(m_half, 2)
                dve.wait_ge(s_rows, 16 * SMALL_LOADS)
                dve.tensor_scalar(fg_t[:, :], ps[0:NH, 0].rearrange("p h f -> p (h f)"), b_fg[:, 0:1], None, ALU.add
                                  ).then_inc(fg_s, 1)
                mix_lo(3, 0, 1)
                rms_inverse(qk_rms, 1)
                dve.wait_ge(fg_s, 4)
                dve.scalar_tensor_tensor(fg_l[:, :], fg_t[:, :], 0.0, fg_l[:, :], ALU.min, ALU.subtract).then_inc(fg_s, 1)
                dve.wait_ge(fg_s, 5)
                dve.tensor_tensor_scan(fg_F[:, :], fg_one[:, :], fg_l[:, :], 0.0, ALU.mult, ALU.add).then_inc(fg_s, 1)
                qk_apply(0, 0)
                qk_lo(0, 0)
                dve.wait_ge(fg_s, 8)
                dve.tensor_tensor(fg4[:, 1], fg_F[:, :], fg4[:, 0].bitcast(F32), ALU.subtract).then_inc(fg_s, 1)
                dve.scalar_tensor_tensor(fg4[:, 3], fg_F[:, :], -1.0, fg4[:, 2].bitcast(F32), ALU.mult, ALU.subtract
                                         ).then_inc(fg_s, 1)
                rms_inverse(qk_rms, 2)
                qk_apply(0, 1)
                mix_lo(4, 0)
                dve.wait_ge(s_spill, 16)
                qk_lo(0, 1)
                v_part(0)
                attention(0, False)
                with dve.Fori(0, NG - 1) as i:
                    hgrn(i, False)
                    attention(i + 1, True)
                hgrn(NG - 1, True)
                for d in range(KD):
                    if d >= 1:
                        add_square(norms[2], d - 1)
                    dve.wait_ge(p_done, d + 1)
                    dve.wait_ge(s_back[d // 2], 16)
                    dve.scalar_tensor_tensor(xT[:, d], pair(d % 4), gate[:, 1, d:d + 1], xT[:, d], ALU.mult, ALU.add
                                             ).then_inc(p_x, 1)
                    if d < 4:
                        mix_lo(N_MIX_IN + d + 4, d % 2, d)
                add_square(norms[2], KD - 1)

            def lower_bounds():
                a, b = cols[:, ROW_LB:ROW_LB + NG], cols[:, ROW_LB + NG:ROW_LB + 2 * NG]
                dve.tensor_tensor(lb[:, :], a, b, ALU.max).then_inc(s_lbe, 1)
                dve.wait_ge(s_lbe, 1)
                dve.tensor_tensor(lb_e[:, 0, :], a, lb[:, :], ALU.subtract)
                dve.tensor_tensor(lb_e[:, 1, :], b, lb[:, :], ALU.subtract).then_inc(s_lbe, 1)
                dve.wait_ge(s_lbe, 3)
                dve.tensor_tensor(lb[:, :], lb_e[:, 0, :], lb_e[:, 1, :], ALU.add).then_inc(s_lbe, 1)
                dve.wait_ge(s_lbe, 4)
                dve.reciprocal(one_less_lb[:, :], lb[:, :]).then_inc(s_lbe, 1)
                dve.wait_ge(s_lbe, 5)
                dve.tensor_tensor(lb[:, :], lb_e[:, 0, :], one_less_lb[:, :], ALU.mult)
                dve.tensor_tensor(one_less_lb[:, :], lb_e[:, 1, :], one_less_lb[:, :], ALU.mult).then_inc(s_lbe, 1)

            dve.wait_ge(s_colsT, 1)
            dve.tensor_copy(cols[:, :], ps[:, 0, 0, 0:N_ROWS]).then_inc(s_cols, 1)
            dve.wait_ge(s_cols, 1)
            lower_bounds()
            dve.wait_ge(s_csilu, 1)
            for k in range(KD):
                add_square(norms[0], k)
                ada_first_add(SH1, k)
            for k in range(KD):
                ada_first_add(SC1, k)
                if k == 2:
                    chunk_lo(ffn1, 0, 0)
                if k == 4:
                    rms_inverse(x_rms, 1)
            mod_read(SH1, 1)
            mod_read(SC1, 1)
            make_amp(0, SC1)
            dve.wait_ge(s_gate, 1)
            norm_apply(norms[0], SH1)
            ffn(ffn1)
            dve.wait_ge(s_gate, 6)
            rms_inverse(x_rms, 2)
            norm_apply(norms[1], SHM)
            mixer_dve()
            rms_inverse(x_rms, 3)
            chunk_lo(ffn2, 0, 0)
            norm_apply(norms[2], SH2)
            ffn(ffn2)


_INS = ['x', 'c', 'w_ada', 'b_ada', 'g_norm1', 'ffn1_w_in', 'ffn1_w_out', 'g_norm_mix', 'w_in_mix', 'b_fgate',
        'q_norm_g', 'k_norm_g', 'attn_out_g', 'hgrn_lb_logits', 'hgrn_out_g', 'w_out_mix', 'g_norm2',
        'ffn2_w_in', 'ffn2_w_out']


def kernel(**inputs):
    import numpy as _np
    import concourse.bacc as _bacc
    from concourse import mybir as _mybir
    from concourse.bass_utils import run_bass_kernel_spmd as _run

    nc = _bacc.Bacc("TRN2", target_bir_lowering=False, num_devices=1)
    arrays, args = {}, []
    for name in _INS:
        a = _np.ascontiguousarray(inputs[name])
        arrays[f"in_{name}_dram"] = a
        args.append(nc.dram_tensor(f"in_{name}_dram", a.shape, _mybir.dt.from_np(a.dtype), kind="ExternalInput").ap())
    shape = inputs['x'].shape
    out = nc.dram_tensor("out_dram", shape, _mybir.dt.float32, kind="ExternalOutput").ap()
    build(nc, *args, out)
    r = _run(nc, [arrays], core_ids=[0])
    return r.results[0]["out_dram"]
```
